# Optimizing a Trainium2 kernel written in Bass

```python
import jax, jax.numpy as jnp
from jax import lax
import numpy as np
import math

D_MODEL = 1024
BATCH = 1
SEQ = 256
DEPTH = 2

GRID_W = 64
NA_HEADS = 8
NA_HEAD_DIM = 64
NA_WIDTH = NA_HEADS * NA_HEAD_DIM
NA_ROWS = 8
NA_COLS = 16
Q_BLOCK_COLS = 16
KEY_BAND_COLS = Q_BLOCK_COLS + NA_COLS
N_COL_BLOCKS = GRID_W // Q_BLOCK_COLS
F_GROUPS = 4
F_GROUP_DIM = 128
F_WIDTH = F_GROUPS * F_GROUP_DIM
IN_COLS = 3 * NA_WIDTH + F_WIDTH + 2 * D_MODEL
D_FF = 2816
RMS_EPS = 1e-6


def rms_norm(x, g):
    xf = x.astype(jnp.float32)
    y = xf * lax.rsqrt(jnp.mean(xf * xf, axis=-1, keepdims=True) + RMS_EPS)
    return (y * g.astype(jnp.float32)).astype(x.dtype)

def swiglu(x, w_in, w_out):
    gu = x @ w_in
    g, u = jnp.split(gu, 2, axis=-1)
    return (jax.nn.silu(g) * u) @ w_out

def neighbourhood_attention(q, k, v, rpb):
    B, T, H, Dh = q.shape
    rows = T // GRID_W
    kh = min(NA_ROWS, rows)
    r = jnp.arange(rows)
    row_start = jnp.clip(r - kh // 2, 0, rows - kh)
    row_idx = row_start[:, None] + jnp.arange(kh)
    j = jnp.arange(N_COL_BLOCKS)
    band_start = jnp.clip(j * Q_BLOCK_COLS - NA_COLS // 2, 0, GRID_W - KEY_BAND_COLS)
    key_col = band_start[:, None] + jnp.arange(KEY_BAND_COLS)
    q_col = j[:, None] * Q_BLOCK_COLS + jnp.arange(Q_BLOCK_COLS)
    win_start = jnp.clip(q_col - NA_COLS // 2, 0, GRID_W - NA_COLS)
    col_ok = (key_col[:, None, :] >= win_start[..., None]) & (
        key_col[:, None, :] < win_start[..., None] + NA_COLS)

    qg = q.reshape(B, rows, N_COL_BLOCKS, Q_BLOCK_COLS, H, Dh)
    kg = k.reshape(B, rows, GRID_W, H, Dh)
    vg = v.reshape(B, rows, GRID_W, H, Dh)
    gi_r = row_idx[:, None, :, None]
    gi_c = key_col[None, :, None, :]
    k_win = kg[:, gi_r, gi_c]
    v_win = vg[:, gi_r, gi_c]

    dr = row_idx - r[:, None] + (NA_ROWS - 1)
    dc = jnp.clip(key_col[:, None, :] - q_col[..., None], -(NA_COLS - 1), NA_COLS - 1) + (NA_COLS - 1)
    bias = rpb[:, dr[:, None, None, :, None], dc[None, :, :, None, :]]
    bias = jnp.transpose(bias, (1, 2, 0, 3, 4, 5)).astype(jnp.float32)

    scale = Dh ** -0.5
    s = jnp.einsum('brjqhd,brjuvhd->brjhquv', qg, k_win).astype(jnp.float32) * scale + bias[None]
    s = jnp.where(col_ok[None, None, :, None, :, None, :], s, -jnp.inf)
    sh = s.shape
    p = jax.nn.softmax(s.reshape(sh[:-2] + (kh * KEY_BAND_COLS,)), axis=-1).reshape(sh)
    o = jnp.einsum('brjhquv,brjuvhd->brjqhd', p.astype(v.dtype), v_win)
    return o.reshape(B, T, H * Dh)

def fourier_mix(u):
    B, T, _ = u.shape
    ug = u.astype(jnp.float32).reshape(B, T, F_GROUPS, F_GROUP_DIM)
    f = jnp.fft.fft2(ug, axes=(1, 3), norm="ortho").real
    return f.reshape(B, T, F_WIDTH).astype(u.dtype)

def mixer(h, w_in, gate_bias, rpb, w_na_out, w_f_out, w_o):
    B, T, _ = h.shape
    z = h @ w_in
    s1 = NA_WIDTH
    q = z[..., :s1]
    k = z[..., s1:2 * s1]
    v = z[..., 2 * s1:3 * s1]
    uf = z[..., 3 * s1:3 * s1 + F_WIDTH]
    ga = z[..., 3 * s1 + F_WIDTH:3 * s1 + F_WIDTH + D_MODEL]
    gf = z[..., 3 * s1 + F_WIDTH + D_MODEL:]
    shp = (B, T, NA_HEADS, NA_HEAD_DIM)
    y_na = neighbourhood_attention(q.reshape(shp), k.reshape(shp), v.reshape(shp), rpb) @ w_na_out
    y_f = fourier_mix(uf) @ w_f_out
    g_na = jax.nn.sigmoid(ga + gate_bias[0])
    g_f = jax.nn.sigmoid(gf + gate_bias[1])
    return (g_na * y_na + g_f * y_f) @ w_o

def first_inputs(seed: int = 0) -> dict:
    key = jax.random.key(seed)
    ks = jax.random.split(key, 20)
    L, D, F = DEPTH, D_MODEL, D_FF

    def w(k, shape, fan_in, mult=1.0):
        return jax.random.normal(k, shape, jnp.float32) * (mult * fan_in ** -0.5)

    def gain(k, shape):
        return 1.0 + 0.05 * jax.random.normal(k, shape, jnp.float32)

    return {
        "x": jax.random.normal(ks[0], (BATCH, SEQ, D), jnp.float32),
        "ffn1_norm": gain(ks[1], (L, D)),
        "ffn1_w_in": w(ks[2], (L, D, 2 * F), D),
        "ffn1_w_out": w(ks[3], (L, F, D), F),
        "mix_norm": gain(ks[4], (L, D)),
        "mix_w_in": w(ks[5], (L, D, IN_COLS), D),
        "mix_gate_bias": 0.1 * jax.random.normal(ks[6], (L, 2, D), jnp.float32),
        "na_rpb": 0.5 * jax.random.normal(ks[7], (L, NA_HEADS, 2 * NA_ROWS - 1, 2 * NA_COLS - 1), jnp.float32),
        "na_w_out": w(ks[8], (L, NA_WIDTH, D), NA_WIDTH),
        "f_w_out": w(ks[9], (L, F_WIDTH, D), F_WIDTH),
        "mix_w_o": w(ks[10], (L, D, D), D),
        "ffn2_norm": gain(ks[11], (L, D)),
        "ffn2_w_in": w(ks[12], (L, D, 2 * F), D),
        "ffn2_w_out": w(ks[13], (L, F, D), F),
        "final_norm": gain(ks[14], (D,)),
    }

def first_block(x, ffn1_norm, ffn1_w_in, ffn1_w_out, mix_norm, mix_w_in, mix_gate_bias,
              na_rpb, na_w_out, f_w_out, mix_w_o, ffn2_norm, ffn2_w_in, ffn2_w_out,
              final_norm):
    for l in range(DEPTH):
        x = x + 0.5 * swiglu(rms_norm(x, ffn1_norm[l]), ffn1_w_in[l], ffn1_w_out[l])
        x = x + mixer(rms_norm(x, mix_norm[l]), mix_w_in[l], mix_gate_bias[l], na_rpb[l],
                      na_w_out[l], f_w_out[l], mix_w_o[l])
        x = x + 0.5 * swiglu(rms_norm(x, ffn2_norm[l]), ffn2_w_in[l], ffn2_w_out[l])
    return rms_norm(x, final_norm)


D_MIX = D_MODEL
N_MIXERS = 4
D_GROUP = D_MIX // N_MIXERS

MLA_HEADS = 4
MLA_Q_RANK = D_MODEL // 4
MLA_KV_RANK = D_MODEL // 8
MLA_NOPE = 64
MLA_ROPE = 32
MLA_V = D_GROUP // MLA_HEADS
ROPE_THETA = 10000.0

CONV_WIDTH = 3
CONV_CH = D_GROUP

POOL_WINDOWS = (2, 4, 8, 16)
POOL_GROUPS = len(POOL_WINDOWS)
POOL_CH = D_GROUP // POOL_GROUPS

SWA_HEADS = 4
SWA_KV_HEADS = 2
SWA_HEAD_DIM = D_GROUP // SWA_HEADS
SWA_WINDOW = 128

BLOCK = 128

D_FF_2 = -(-8 * D_MODEL // (3 * 256)) * 256


IN_SPLITS = (MLA_Q_RANK, MLA_KV_RANK, MLA_ROPE,
             CONV_CH, CONV_CH, CONV_CH,
             D_GROUP,
             SWA_HEADS * SWA_HEAD_DIM,
             SWA_KV_HEADS * SWA_HEAD_DIM,
             SWA_KV_HEADS * SWA_HEAD_DIM)
D_IN = sum(IN_SPLITS)


def _split_points():
    pts, acc = [], 0
    for w in IN_SPLITS[:-1]:
        acc += w
        pts.append(acc)
    return pts

def _alibi_slopes(n):
    return np.asarray([2.0 ** (-8.0 * (i + 1) / n) for i in range(n)], dtype=np.float32)

def rmsnorm(x, g):
    xf = x.astype(jnp.float32)
    y = xf * lax.rsqrt(jnp.mean(xf * xf, axis=-1, keepdims=True) + RMS_EPS)
    return (y * g.astype(jnp.float32)).astype(x.dtype)

def rope_tables(seq, dim, dtype):
    inv = 1.0 / (ROPE_THETA ** (jnp.arange(0, dim, 2, dtype=jnp.float32) / dim))
    ang = jnp.arange(seq, dtype=jnp.float32)[:, None] * inv[None, :]
    return jnp.cos(ang).astype(dtype), jnp.sin(ang).astype(dtype)

def apply_rope(x, cos, sin):
    x1, x2 = jnp.split(x, 2, axis=-1)
    c = cos[:, None, :]
    s = sin[:, None, :]
    return jnp.concatenate([x1 * c - x2 * s, x1 * s + x2 * c], axis=-1)

def mla_attention(c_q, c_kv, k_r, q_norm_g, kv_norm_g, w_uq, w_ukv, cos, sin):
    b, s, _ = c_q.shape
    dqk = MLA_NOPE + MLA_ROPE
    q = (rmsnorm(c_q, q_norm_g) @ w_uq).reshape(b, s, MLA_HEADS, dqk)
    q_nope, q_rot = q[..., :MLA_NOPE], q[..., MLA_NOPE:]
    q_rot = apply_rope(q_rot, cos, sin)
    kv = (rmsnorm(c_kv, kv_norm_g) @ w_ukv).reshape(b, s, MLA_HEADS, MLA_NOPE + MLA_V)
    k_nope, v = kv[..., :MLA_NOPE], kv[..., MLA_NOPE:]
    k_rot = apply_rope(k_r[:, :, None, :], cos, sin)
    k = jnp.concatenate([k_nope, jnp.broadcast_to(k_rot, (b, s, MLA_HEADS, MLA_ROPE))], axis=-1)
    q = jnp.concatenate([q_nope, q_rot], axis=-1) * (1.0 / math.sqrt(dqk))
    nb = s // BLOCK
    qb = q.reshape(b, nb, BLOCK, MLA_HEADS, dqk).transpose(1, 0, 2, 3, 4)
    key_pos = jnp.arange(s)

    def one_block(args):
        q_blk, i = args
        sc = jnp.einsum('bqhd,bkhd->bhqk', q_blk, k).astype(jnp.float32)
        q_pos = i * BLOCK + jnp.arange(BLOCK)
        causal = key_pos[None, :] <= q_pos[:, None]
        sc = jnp.where(causal[None, None], sc, -jnp.inf)
        p = jax.nn.softmax(sc, axis=-1).astype(v.dtype)
        return jnp.einsum('bhqk,bkhd->bqhd', p, v)

    out = lax.map(one_block, (qb, jnp.arange(nb)))
    return out.transpose(1, 0, 2, 3, 4).reshape(b, s, MLA_HEADS * MLA_V)

def short_gated_conv(gate_b, gate_c, u, conv_w):
    z = gate_c * u
    y = lax.conv_general_dilated(
        z, conv_w[:, None, :].astype(z.dtype), window_strides=(1,),
        padding=[(CONV_WIDTH - 1, 0)], dimension_numbers=('NWC', 'WIO', 'NWC'),
        feature_group_count=CONV_CH)
    return gate_b * y

def multiscale_pool(u, pool_w, pool_scale):
    b, s, _ = u.shape
    uf = u.astype(jnp.float32)
    cs = jnp.cumsum(uf, axis=1)
    pos = jnp.arange(s)
    outs = []
    for g, w in enumerate(POOL_WINDOWS):
        cs_g = cs[:, :, g * POOL_CH:(g + 1) * POOL_CH]
        lag = jnp.pad(cs_g, ((0, 0), (w, 0), (0, 0)))[:, :s]
        count = jnp.minimum(pos + 1, w).astype(jnp.float32)[None, :, None]
        outs.append((cs_g - lag) / count)
    pooled = jnp.stack(outs, axis=2) - uf.reshape(b, s, POOL_GROUPS, POOL_CH)
    mixed = jnp.einsum('bsgc,gcd->bsgd', pooled.astype(u.dtype), pool_w)
    return mixed.reshape(b, s, D_GROUP) * pool_scale

def swa_sink_attention(q, k, v, sinks, slopes):
    b, s, _, hd = q.shape
    grp = SWA_HEADS // SWA_KV_HEADS
    nb = s // BLOCK
    qb = q.reshape(b, nb, BLOCK, SWA_KV_HEADS, grp, hd)
    kb = k.reshape(b, nb, BLOCK, SWA_KV_HEADS, hd)
    vb = v.reshape(b, nb, BLOCK, SWA_KV_HEADS, hd)

    def with_prev(t):
        prev = jnp.pad(t, ((0, 0), (1, 0), (0, 0), (0, 0), (0, 0)))[:, :nb]
        return jnp.concatenate([prev, t], axis=2)

    kk, vv = with_prev(kb), with_prev(vb)
    sc = jnp.einsum('bnqkgd,bnskd->bnkgqs', qb, kk).astype(jnp.float32) * (1.0 / math.sqrt(hd))
    blk = jnp.arange(nb)[:, None] * BLOCK
    q_pos = blk + jnp.arange(BLOCK)[None, :]
    k_pos = blk - BLOCK + jnp.arange(2 * BLOCK)[None, :]
    dist = q_pos[:, :, None] - k_pos[:, None, :]
    valid = (dist >= 0) & (dist < SWA_WINDOW) & (k_pos[:, None, :] >= 0)
    sl = jnp.asarray(slopes).reshape(SWA_KV_HEADS, grp)
    bias = -sl[None, None, :, :, None, None] * dist.astype(jnp.float32)[None, :, None, None, :, :]
    sc = jnp.where(valid[None, :, None, None], sc + bias, -jnp.inf)
    sink = jnp.broadcast_to(
        sinks.astype(jnp.float32).reshape(SWA_KV_HEADS, grp)[None, None, :, :, None, None],
        sc.shape[:-1] + (1,))
    p = jax.nn.softmax(jnp.concatenate([sc, sink], axis=-1), axis=-1)[..., :-1].astype(v.dtype)
    out = jnp.einsum('bnkgqs,bnskd->bnqkgd', p, vv)
    return out.reshape(b, s, SWA_HEADS * hd)

def second_inputs(seed: int = 0) -> dict:
    key = jax.random.key(seed)
    ks = jax.random.split(key, 17)
    f32 = jnp.float32

    def dense(k, shape, fan_in):
        return jax.random.normal(k, shape, f32) * fan_in ** -0.5

    def gain(k, shape):
        return 1.0 + 0.05 * jax.random.normal(k, shape, f32)

    return {
        "x": jax.random.normal(ks[0], (BATCH, SEQ, D_MODEL), f32),
        "attn_norm": gain(ks[1], (DEPTH, D_MODEL)),
        "w_in": dense(ks[2], (DEPTH, D_MODEL, D_IN), D_MODEL),
        "mla_q_norm": gain(ks[3], (DEPTH, MLA_Q_RANK)),
        "w_uq": dense(ks[4], (DEPTH, MLA_Q_RANK, MLA_HEADS * (MLA_NOPE + MLA_ROPE)), MLA_Q_RANK),
        "mla_kv_norm": gain(ks[5], (DEPTH, MLA_KV_RANK)),
        "w_ukv": dense(ks[6], (DEPTH, MLA_KV_RANK, MLA_HEADS * (MLA_NOPE + MLA_V)), MLA_KV_RANK),
        "conv_w": dense(ks[7], (DEPTH, CONV_WIDTH, CONV_CH), CONV_WIDTH),
        "pool_w": dense(ks[8], (DEPTH, POOL_GROUPS, POOL_CH, POOL_CH), POOL_CH),
        "pool_scale": gain(ks[9], (DEPTH, D_GROUP)),
        "swa_sinks": 0.5 * jax.random.normal(ks[10], (DEPTH, SWA_HEADS), f32),
        "mix_norm": gain(ks[11], (DEPTH, D_MIX)),
        "w_o": dense(ks[12], (DEPTH, D_MIX, D_MODEL), D_MIX),
        "ffn_norm": gain(ks[13], (DEPTH, D_MODEL)),
        "w_gate_up": dense(ks[14], (DEPTH, D_MODEL, 2 * D_FF_2), D_MODEL),
        "w_down": dense(ks[15], (DEPTH, D_FF_2, D_MODEL), D_FF_2),
        "final_norm": gain(ks[16], (D_MODEL,)),
    }

def second_block(x, attn_norm, w_in, mla_q_norm, w_uq, mla_kv_norm, w_ukv, conv_w, pool_w,
              pool_scale, swa_sinks, mix_norm, w_o, ffn_norm, w_gate_up, w_down, final_norm):
    b, s, _ = x.shape
    cos, sin = rope_tables(s, MLA_ROPE, x.dtype)
    slopes = _alibi_slopes(SWA_HEADS)
    pts = _split_points()
    for l in range(DEPTH):
        h = rmsnorm(x, attn_norm[l])
        proj = h @ w_in[l]
        (c_q, c_kv, k_r, g_b, g_c, u_conv, u_pool,
         q_sw, k_sw, v_sw) = jnp.split(proj, pts, axis=-1)
        y_a = mla_attention(c_q, c_kv, k_r, mla_q_norm[l], mla_kv_norm[l],
                            w_uq[l], w_ukv[l], cos, sin)
        y_b = short_gated_conv(g_b, g_c, u_conv, conv_w[l])
        y_c = multiscale_pool(u_pool, pool_w[l], pool_scale[l])
        y_d = swa_sink_attention(q_sw.reshape(b, s, SWA_HEADS, SWA_HEAD_DIM),
                                 k_sw.reshape(b, s, SWA_KV_HEADS, SWA_HEAD_DIM),
                                 v_sw.reshape(b, s, SWA_KV_HEADS, SWA_HEAD_DIM),
                                 swa_sinks[l], slopes)
        groups = jnp.stack([y_a, y_b, y_c, y_d], axis=2)
        gf = groups.astype(jnp.float32)
        gf = gf * lax.rsqrt(jnp.mean(gf * gf, axis=-1, keepdims=True) + RMS_EPS)
        mixed = (gf.reshape(b, s, D_MIX) * mix_norm[l].astype(jnp.float32)).astype(x.dtype)
        x = x + mixed @ w_o[l]
        h2 = rmsnorm(x, ffn_norm[l])
        gate, up = jnp.split(h2 @ w_gate_up[l], 2, axis=-1)
        x = x + (jax.nn.silu(gate) * up) @ w_down[l]
    return rmsnorm(x, final_norm)


def setup_inputs(seed=0):
    out = dict(first_inputs(seed))
    for name, value in second_inputs(seed + 1).items():
        if name != "x":
            out[name + "_2"] = value
    return out


def reference(
    x, ffn1_norm, ffn1_w_in, ffn1_w_out, mix_norm, mix_w_in, mix_gate_bias, na_rpb, na_w_out,
    f_w_out, mix_w_o, ffn2_norm, ffn2_w_in, ffn2_w_out, final_norm, attn_norm_2, w_in_2,
    mla_q_norm_2, w_uq_2, mla_kv_norm_2, w_ukv_2, conv_w_2, pool_w_2, pool_scale_2, swa_sinks_2,
    mix_norm_2, w_o_2, ffn_norm_2, w_gate_up_2, w_down_2, final_norm_2,
):
    x = first_block(
        x, ffn1_norm, ffn1_w_in, ffn1_w_out, mix_norm, mix_w_in, mix_gate_bias, na_rpb,
        na_w_out, f_w_out, mix_w_o, ffn2_norm, ffn2_w_in, ffn2_w_out, final_norm,
    )
    return second_block(
        x, attn_norm_2, w_in_2, mla_q_norm_2, w_uq_2, mla_kv_norm_2, w_ukv_2, conv_w_2,
        pool_w_2, pool_scale_2, swa_sinks_2, mix_norm_2, w_o_2, ffn_norm_2, w_gate_up_2,
        w_down_2, final_norm_2,
    )


_drawn_inputs = setup_inputs


def setup_inputs(seed=0):
    import zlib

    import numpy as np

    out = dict(_drawn_inputs(seed))
    spreads = {}
    factors = {}
    for name, (base, spread) in spreads.items():
        noise = np.random.default_rng([zlib.crc32(name.encode()), seed]).standard_normal(out[name].shape)
        drawn = base * np.exp(spread * noise) if base else spread * noise
        out[name] = __import__('jax').numpy.asarray(drawn.astype(out[name].dtype))
    for name, factor in factors.items():
        out[name] = (out[name] * factor).astype(out[name].dtype)
    return out
```

```python
from contextlib import ExitStack

import numpy as np

import concourse.bass as bass
from concourse import mybir

F32 = mybir.dt.float32
F32R = mybir.dt.float32r
ACT = mybir.ActivationFunctionType
ALU = mybir.AluOpType
AX = mybir.AxisListType

P = 128
D = 1024
T = 256
TT = T // P
KC = D // P
DEPTH = 2
EPS = 1e-6
F = 2816
FB = 256
STEPS = F // FB
BANK = 512
UNIT = 4 * BANK
SLOTS = 3

GRID_W, NA_H, NA_D, NA_COLS = 64, 8, 64, 16
GRID_H = T // GRID_W
RPB_R, RPB_C = 15, 31
NA_SCALE = NA_D ** -0.5
NA_DR = 2 * GRID_H - 1
MASKED = -1e30
FG, FC = 4, 128
A_IN = 4096

MLA_H, NOPE, ROPE, MLA_V = 4, 64, 32, 64
MLA_D = NOPE + ROPE
QR, KVR = 256, 128
C_COLS = QR + KVR + ROPE
SW_H, SW_KV, SW_D = 4, 2, 64
WINDOWS = (2, 4, 8, 16)
PC = 64
CONV_W = 3
GD = 256
B_IN = 1952

FFN_ROUNDS = STEPS
MIXA_ROUNDS = 8
MIXB_ROUNDS = 5
A_ROUNDS = 2 * FFN_ROUNDS + MIXA_ROUNDS
B_ROUNDS = FFN_ROUNDS + MIXB_ROUNDS
B_START = DEPTH * A_ROUNDS

CA_DFT_T, CA_DFT_C, CA_MASK = 0, TT * 2 * T, TT * 2 * T + 2 * FC
CA_COLS = CA_MASK + T
CB_ROPE = 0
CB_CAUSAL = CB_ROPE + TT * 2 * ROPE
CB_SWA = CB_CAUSAL + T
CB_POOL = CB_SWA + 3 * BANK
CB_CONV = CB_POOL + len(WINDOWS) * 3 * P
CB_COLS = CB_CONV + 5 * P


def first_constants():
    out = np.zeros((P, CA_COLS), np.float32)
    t = np.arange(T)
    angle = 2 * np.pi * np.outer(t, t) / T
    norm = 1.0 / np.sqrt(T * FC)
    table = np.concatenate([np.cos(angle) * norm, np.sin(angle) * norm], 1)
    out[:, CA_DFT_T:CA_DFT_C] = table.reshape(TT, P, 2 * T).transpose(1, 0, 2).reshape(P, -1)
    c = np.arange(FC)
    angle = 2 * np.pi * np.outer(c, c) / FC
    out[:, CA_DFT_C:CA_MASK] = np.concatenate([np.cos(angle), -np.sin(angle)], 1)
    col = np.arange(P) % GRID_W
    start = np.clip(col - NA_COLS // 2, 0, GRID_W - NA_COLS)[:, None]
    key = np.arange(T)[None, :] % GRID_W
    out[:, CA_MASK:] = np.where((key >= start) & (key < start + NA_COLS), 0.0, MASKED)
    return out


def second_constants():
    out = np.zeros((P, CB_COLS), np.float32)
    inv = (1.0 / (np.float32(10000.0) ** (np.arange(0, ROPE, 2, dtype=np.float32) / np.float32(ROPE))))
    ang = np.arange(T, dtype=np.float32)[:, None] * inv.astype(np.float32)[None, :]
    cos, sin = np.cos(ang), np.sin(ang)
    rope = np.concatenate([cos, cos, -sin, sin], 1)
    out[:, CB_ROPE:CB_CAUSAL] = rope.reshape(TT, P, 2 * ROPE).transpose(1, 0, 2).reshape(P, -1)
    q, k = np.arange(P)[:, None], np.arange(T)[None, :]
    out[:, CB_CAUSAL:CB_SWA] = np.where(k <= q + P, 0.0, MASKED)
    slopes = [2.0 ** (-8.0 * (h + 1) / SW_H) for h in range(SW_H)]
    dist = (q + P) - k
    for h in range(SW_H):
        near = (dist >= 0) & (dist < P)
        full = np.where(near, -slopes[h] * dist, MASKED)
        own = full[:, P:]
        out[:, CB_SWA + h * P:CB_SWA + (h + 1) * P] = own
        out[:, CB_SWA + BANK + h * T:CB_SWA + BANK + (h + 1) * T] = full
    s, t = np.arange(T)[:, None], np.arange(T)[None, :]
    for g, w in enumerate(WINDOWS):
        band = ((s <= t) & (s > t - w)) / np.minimum(t + 1, w) - (s == t)
        at = CB_POOL + g * 3 * P
        out[:, at:at + T] = band[:P]
        out[:, at + T:at + T + P] = band[P:, P:]
    s, t = np.arange(P)[:, None], np.arange(P)[None, :]
    for n, m in enumerate([t == s + 2, t == s + 1, t == s, t + P == s + 2, t + P == s + 1]):
        out[:, CB_CONV + n * P:CB_CONV + (n + 1) * P] = m
    return out


class Signals:

    def __init__(self, sem):
        self.consts_a_landed = sem("consts_a_landed")
        self.consts_b_landed = sem("consts_b_landed")
        self.x_landed = sem("x_landed")
        self.rpb_spread = sem("rpb_spread")
        self.bias_landed = sem("bias_landed")
        self.gain_a_landed = sem("gain_a_landed")
        self.gain_m_landed = sem("gain_m_landed")
        self.gain_f_landed = sem("gain_f_landed")
        self.gate_bias_landed = sem("gate_bias_landed")
        self.small_landed = sem("small_landed")
        self.ident_zero = sem("ident_zero")
        self.ident_ready = sem("ident_ready")
        self.half_ready = sem("half_ready")
        self.bias_masked = sem("bias_masked")
        self.w_hi_ready = sem("w_hi_ready")
        self.w_lo_ready = sem("w_lo_ready")
        self.unit_done = sem("unit_done")
        self.x_written0 = sem("x_written0")
        self.x_written1 = sem("x_written1")
        self.sq_ready = sem("sq_ready")
        self.ms_ready = sem("ms_ready")
        self.rstd_ready = sem("rstd_ready")
        self.xn_ready = sem("xn_ready")
        self.tr_done = sem("tr_done")
        self.xT_hi_ready = sem("xT_hi_ready")
        self.xT_lo_ready = sem("xT_lo_ready")
        self.ffn_t0_done = sem("ffn_t0_done")
        self.silu_ready = sem("silu_ready")
        self.act_ready = sem("act_ready")
        self.actT_tr = sem("actT_tr")
        self.actT_hi = sem("actT_hi")
        self.actT_lo = sem("actT_lo")
        self.mixa_t0_done = sem("mixa_t0_done")
        self.qk_sb = sem("qk_sb")
        self.qkT_tr = sem("qkT_tr")
        self.qkT_sb = sem("qkT_sb")
        self.v_sb = sem("v_sb")
        self.uf_sb = sem("uf_sb")
        self.gate_added = sem("gate_added")
        self.gate_sig = sem("gate_sig")
        self.na_scores = sem("na_scores")
        self.na_biased = sem("na_biased")
        self.na_negmax = sem("na_negmax")
        self.na_exp = sem("na_exp")
        self.naPT_done = sem("naPT_done")
        self.naPT_sb = sem("naPT_sb")
        self.na_o_done = sem("na_o_done")
        self.na_rinv = sem("na_rinv")
        self.na_o_sb = sem("na_o_sb")
        self.oT_tr = sem("oT_tr")
        self.oT_hi = sem("oT_hi")
        self.oT_lo = sem("oT_lo")
        self.dft1_done = sem("dft1_done")
        self.dft1_sb = sem("dft1_sb")
        self.dft2_done = sem("dft2_done")
        self.fT_hi = sem("fT_hi")
        self.fT_lo = sem("fT_lo")
        self.mix_f_ready = sem("mix_f_ready")
        self.mix_na_ready = sem("mix_na_ready")
        self.mixb_t0_done = sem("mixb_t0_done")
        self.c_sb = sem("c_sb")
        self.c_sq = sem("c_sq")
        self.c_ms = sem("c_ms")
        self.c_rstd = sem("c_rstd")
        self.cn_ready = sem("cn_ready")
        self.cT_tr = sem("cT_tr")
        self.cT_hi = sem("cT_hi")
        self.cT_lo = sem("cT_lo")
        self.sw_sb = sem("sw_sb")
        self.swqT_tr = sem("swqT_tr")
        self.swqT_sb = sem("swqT_sb")
        self.swkT_tr = sem("swkT_tr")
        self.swkT_sb = sem("swkT_sb")
        self.rope_a = sem("rope_a")
        self.q_sb = sem("q_sb")
        self.krot_a = sem("krot_a")
        self.krot_ready = sem("krot_ready")
        self.knope_sb = sem("knope_sb")
        self.mlaT_tr = sem("mlaT_tr")
        self.mlaT_q_sb = sem("mlaT_q_sb")
        self.mlaT_k_sb = sem("mlaT_k_sb")
        self.sw_scores = sem("sw_scores")
        self.sw_biased = sem("sw_biased")
        self.sw_max = sem("sw_max")
        self.sw_maxed = sem("sw_maxed")
        self.sw_sinkarg = sem("sw_sinkarg")
        self.sw_exp = sem("sw_exp")
        self.sw_sinkexp = sem("sw_sinkexp")
        self.swPT_done = sem("swPT_done")
        self.swPT_sb = sem("swPT_sb")
        self.sw_o_done = sem("sw_o_done")
        self.sw_den = sem("sw_den")
        self.sw_rinv = sem("sw_rinv")
        self.sw_o_sb = sem("sw_o_sb")
        self.mla_scores = sem("mla_scores")
        self.mla_biased = sem("mla_biased")
        self.mla_negmax = sem("mla_negmax")
        self.mla_exp = sem("mla_exp")
        self.mlaPT_done = sem("mlaPT_done")
        self.mlaPT_sb = sem("mlaPT_sb")
        self.mla_o_done = sem("mla_o_done")
        self.mla_rinv = sem("mla_rinv")
        self.mla_o_sb = sem("mla_o_sb")
        self.gates_sb = sem("gates_sb")
        self.z_ready = sem("z_ready")
        self.up_sb = sem("up_sb")
        self.zw_ready = sem("zw_ready")
        self.conv_done = sem("conv_done")
        self.conv_sb = sem("conv_sb")
        self.pooled_done = sem("pooled_done")
        self.pooled_hi = sem("pooled_hi")
        self.pooled_lo = sem("pooled_lo")
        self.pool_sb = sem("pool_sb")
        self.gsq_ready = sem("gsq_ready")
        self.gms_ready = sem("gms_ready")
        self.grstd_ready = sem("grstd_ready")
        self.final_done = sem("final_done")
        self.out_stored = sem("out_stored")


def build(nc, a, out):
    with ExitStack() as ctx:
        def sb(name, shape, dt=F32):
            return ctx.enter_context(nc.sbuf_tensor(name, shape, dt))

        def psum(name):
            return ctx.enter_context(nc.psum_tensor(name, [P, BANK], F32))

        s = Signals(lambda name: ctx.enter_context(nc.semaphore(name)))
        raw_landed = [ctx.enter_context(nc.semaphore(f"raw_landed{i}")) for i in range(SLOTS)]
        x_written = [s.x_written0, s.x_written1]

        raw = sb("raw", [P, SLOTS, UNIT])
        whi = sb("whi", [P, SLOTS, UNIT], F32R)
        wlo = sb("wlo", [P, SLOTS, UNIT], F32R)
        x = sb("x", [P, TT, D])
        xn = sb("xn", [P, TT, D])
        xTh = sb("xTh", [P, KC, T], F32R)
        xTl = sb("xTl", [P, KC, T], F32R)
        bTh = sb("bTh", [P, 8, T], F32R)
        bTl = sb("bTl", [P, 8, T], F32R)
        gain_a = sb("gain_a", [P, D])
        gain_m = sb("gain_m", [P, D])
        gain_f = sb("gain_f", [P, D])
        ident = sb("ident", [P, P])
        neghalf = sb("neghalf", [P, 8])
        eps = sb("eps", [P, 8])
        ss = sb("ss", [P, TT])
        ms = sb("ms", [P, TT])
        rstd = sb("rstd", [P, TT])
        consts_a = sb("consts_a", [P, CA_COLS])
        shared = sb("shared", [P, TT * NA_H * T])
        bias = shared[:, :].rearrange("p (t h k) -> p t h k", t=TT, h=NA_H)
        consts_b = shared
        work = sb("work", [P, 13 * 1024])

        def area(at, *shape):
            n = int(np.prod(shape))
            v = work[:, at:at + n]
            if len(shape) == 2:
                v = v.rearrange("p (a b) -> p a b", a=shape[0])
            if len(shape) == 3:
                v = v.rearrange("p (a b c) -> p a b c", a=shape[0], b=shape[1])
            return v

        sg, act = area(12288, TT, FB), area(12800, TT, FB)

        gate = area(0, TT, 2 * D)
        q_nat, k_nat = area(4096, TT, BANK), area(5120, TT, BANK)
        o_nat = q_nat
        v_nat, uf = area(6144, TT, BANK), area(7168, TT, BANK)
        qT, kT = area(8192, 4, T), area(9216, 4, T)
        probs, probsT = area(10240, 2, BANK), area(11264, 2, BANK)
        dft = area(12288, BANK)
        oTh, oTl, fTh, fTl = bTh[:, 0:4, :], bTl[:, 0:4, :], bTh[:, 4:8, :], bTl[:, 4:8, :]
        na_neg = sb("na_neg", [P, 8, 2])
        na_sum = sb("na_sum", [P, TT, NA_H])
        na_inv = sb("na_inv", [P, TT, NA_H])

        y = xn
        gates, sw_nat = area(0, TT, BANK), area(1024, TT, BANK)
        c_nat = area(2048, TT, C_COLS)
        z = area(2048, TT, GD)
        small = area(2880, QR + KVR + CONV_W * GD + GD + SW_H)
        kvg_at, convw_at = QR, QR + KVR
        pscale_at = convw_at + CONV_W * GD
        sink_at = pscale_at + GD
        mqT, mkT = area(4352, MLA_H, T), area(5376, MLA_H, T)
        sqT = area(6400, SW_H, T)
        mP, mPT, sP, sPT = (area(7424 + i * BANK, BANK) for i in range(4))
        skT = area(9472, SW_KV, T)
        mq, mk = area(9984, TT, MLA_H * MLA_D), area(10752, TT, MLA_H * MLA_D)
        zw = area(9984, TT, CONV_W, GD)
        mv = area(11520, TT, MLA_H * MLA_V)
        ropeA, ropeB = area(12032, TT, MLA_H, ROPE), area(12288, TT, MLA_H, ROPE)
        up = area(12032, TT, GD)
        krA, krB = area(12544, TT, ROPE), area(12608, TT, ROPE)
        unused = (sqT, mqT)
        cTh, cTl = bTh[:, 0:3, :], bTl[:, 0:3, :]
        plTh, plTl = bTh[:, 4:8, :], bTl[:, 4:8, :]
        c_ss, c_m, c_r = sb("c_ss", [P, TT, 2]), sb("c_m", [P, TT, 2]), sb("c_r", [P, TT, 2])
        m_neg, m_sum, m_inv = sb("m_neg", [P, 3, 4]), sb("m_sum", [P, TT, 4]), sb("m_inv", [P, TT, 4])
        s_max, s_neg, s_arg, s_snk = (sb(n, [P, 3, 4]) for n in ("s_max", "s_neg", "s_arg", "s_snk"))
        s_sum, s_den, s_inv = (sb(n, [P, TT, 4]) for n in ("s_sum", "s_den", "s_inv"))
        g_ss, g_m, g_r = (sb(n, [P, TT, 4]) for n in ("g_ss", "g_m", "g_r"))

        pg = [[psum(f"pg{i}{t}") for t in range(TT)] for i in range(2)]
        acc = [psum(f"acc{i}") for i in range(4)]

        spread = nc.dram_tensor("rpb_spread", (DEPTH, GRID_W, NA_H, NA_DR * GRID_W), F32, kind="Internal").ap()

        causal = consts_b[:, CB_CAUSAL:CB_CAUSAL + T]

        def rope_table(t, which):
            at = CB_ROPE + (2 * t + which) * ROPE
            return consts_b[:, at:at + ROPE]

        def f32(ap):
            return ap.bitcast(F32)

        def tok(t):
            return slice(t * P, (t + 1) * P)

        def ffn_stages_a(l):
            return ((A_ROUNDS * l, 2 * l, 3 * l, 4 * l), (A_ROUNDS * l + FFN_ROUNDS + MIXA_ROUNDS, 2 * l + 1, 3 * l + 2, 4 * l + 3))

        def mixa_stage(l):
            return A_ROUNDS * l + FFN_ROUNDS, 3 * l + 1, 4 * l + 1

        def mixb_stage(l):
            return B_START + B_ROUNDS * l, 7 + 2 * l, 8 + 3 * l

        def ffn_stage_b(l):
            return B_START + B_ROUNDS * l + MIXB_ROUNDS, 4 + l, 7 + 2 * l + 1, 8 + 3 * l + 2

        units_b = ((4, P, 0, 0), (2, T, 0, 1), (2, T, 2, 1))

        def unit(slot, rnd):
            return SLOTS * rnd + slot

        block = ctx.enter_context(nc.Block())

        @block.sync
        def _(sp):
            def dram(t, offset, *dims):
                return bass.AP(tensor=a[t].tensor, offset=offset, ap=[list(d) for d in dims])

            def load(slot, rnd, pieces):
                sp.wait_ge(s.w_lo_ready, unit(slot, rnd) + 1)
                assert len(pieces) == 2
                for dst, src in pieces:
                    sp.dma_start(dst, src).then_inc(raw_landed[slot], 16)

            def rows(name, offset, pitch, slot, at, k, n):
                dst = raw[:, slot, at:at + k * n].rearrange("p (k n) -> p k n", k=k)
                return dst, dram(name, offset, (pitch, P), (pitch * P, k), (1, n))

            def broadcast(dst, name, offset, n, sem):
                sp.dma_start(dst, dram(name, offset, (0, P), (1, n))).then_inc(sem, 16)

            def block_units(name, l, pitch, width, col, n, first, rnd):
                for half in range(2):
                    i = first + half
                    at = l * (D * pitch) + half * (4 * P * pitch) + col
                    load(i % SLOTS, rnd + i // SLOTS,
                         [rows(name, at + 2 * u * P * pitch, pitch, i % SLOTS, 2 * u * n, 2, n) for u in range(2)])

            def ffn(w_in, w_out, l, rnd, after_first=None):
                def gate_up(slots, rnds, j):
                    for half in range(2):
                        at = l * (D * 2 * F) + half * (4 * P * 2 * F) + j * FB
                        dst = raw[:, slots[half], :].rearrange("p (k n) -> p k n", k=4)
                        load(slots[half], rnds[half],
                             [(dst[:, :, u * FB:(u + 1) * FB], dram(w_in, at + u * F, (2 * F, P), (2 * F * P, 4), (1, FB)))
                              for u in range(2)])

                def down(slot, r, j):
                    at = l * (F * D) + j * (FB * D)
                    load(slot, r, [rows(w_out, at + k * P * D, D, slot, k * D, 1, D) for k in range(2)])

                gate_up((0, 1), (rnd, rnd), 0)
                if after_first:
                    after_first()
                with sp.Fori(0, STEPS - 1) as j:
                    gate_up((2, 0), (rnd + j, rnd + j + 1), j + 1)
                    down(1, rnd + j + 1, j)
                down(2, rnd + STEPS - 1, STEPS - 1)

            sp.dma_start(x[:, :, :], dram("x", 0, (D, P), (P * D, TT), (1, D))).then_inc(s.x_landed, 16)

            with sp.Fori(0, DEPTH) as l:
                (r1, _, _, _), (r2, _, _, _) = ffn_stages_a(l)
                sp.wait_ge(s.xn_ready, 8 * l + 1)
                broadcast(gain_a[:, :], "ffn1_norm", l * D, D, s.gain_a_landed)

                def parameters():
                    broadcast(gain_m[:, :], "mix_norm", l * D, D, s.gain_m_landed)
                    broadcast(gain_f[:, :], "ffn2_norm", l * D, D, s.gain_f_landed)
                    for t in range(TT):
                        broadcast(gate[:, t, :], "mix_gate_bias", l * 2 * D, 2 * D, s.gate_bias_landed)
                    sp.dma_start(consts_a[:, :], a["consts_a"]).then_inc(s.consts_a_landed, 16)
                    sp.wait_ge(s.rpb_spread, 16 * DEPTH * NA_DR)
                    for t in range(TT):
                        for r in range(2):
                            first = GRID_H - 1 - (2 * t + r)
                            src = bass.AP(tensor=spread.tensor,
                                          offset=l * (GRID_W * NA_H * NA_DR * GRID_W) + first * GRID_W,
                                          ap=[[NA_H * NA_DR * GRID_W, GRID_W], [NA_DR * GRID_W, NA_H], [1, T]])
                            sp.dma_start(bias[GRID_W * r:GRID_W * (r + 1), t, :, :], src).then_inc(s.bias_landed, 16)

                ffn("ffn1_w_in", "ffn1_w_out", l, r1, parameters)
                rm, _, _ = mixa_stage(l)
                for b, col in enumerate((0, 512, 1024, 1536, 2048, 2560, 3072, 3584)):
                    block_units("mix_w_in", l, A_IN, 0, col, BANK, 2 * b, rm)
                for i, name in ((16, "f_w_out"), (17, "f_w_out"), (18, "na_w_out"), (19, "na_w_out")):
                    n = i % 2
                    load(i % SLOTS, rm + i // SLOTS,
                         [rows(name, l * (BANK * D) + 2 * u * P * D + n * BANK, D, i % SLOTS, 2 * u * BANK, 2, BANK)
                          for u in range(2)])
                for n in range(2):
                    block_units("mix_w_o", l, D, 0, n * BANK, BANK, 20 + 2 * n, rm)
                ffn("ffn2_w_in", "ffn2_w_out", l, r2)

            sp.wait_ge(s.xn_ready, 8 * DEPTH + 1)
            broadcast(gain_m[:, :], "final_norm", 0, D, s.gain_m_landed)
            sp.dma_start(consts_b[:, 0:CB_COLS], a["consts_b"]).then_inc(s.consts_b_landed, 16)

            with sp.Fori(0, DEPTH) as l:
                rm, _, _ = mixb_stage(l)
                sp.wait_ge(s.xn_ready, 8 * DEPTH + 6 * l + 1)
                broadcast(gain_a[:, :], "attn_norm_2", l * D, D, s.gain_a_landed)
                block_units("w_in_2", l, B_IN, 0, 0, C_COLS, 0, rm)
                broadcast(gain_f[:, :], "ffn_norm_2", l * D, D, s.gain_f_landed)
                broadcast(small[:, 0:QR], "mla_q_norm_2", l * QR, QR, s.small_landed)
                broadcast(small[:, kvg_at:kvg_at + KVR], "mla_kv_norm_2", l * KVR, KVR, s.small_landed)
                broadcast(small[:, convw_at:convw_at + CONV_W * GD], "conv_w_2", l * CONV_W * GD, CONV_W * GD, s.small_landed)
                broadcast(small[:, pscale_at:pscale_at + GD], "pool_scale_2", l * GD, GD, s.small_landed)
                broadcast(small[:, sink_at:sink_at + SW_H], "swa_sinks_2", l * SW_H, SW_H, s.small_landed)
                block_units("w_in_2", l, B_IN, 0, 1440, BANK, 2, rm)
                nq = MLA_H * MLA_D
                load(4 % SLOTS, rm + 1, [rows("w_uq_2", l * (QR * nq) + k * P * nq, nq, 1, k * nq, 1, nq) for k in range(2)])
                load(5 % SLOTS, rm + 1, [rows("w_ukv_2", l * (KVR * BANK) + u * 256, BANK, 2, u * 256, 1, 256) for u in range(2)])
                block_units("w_in_2", l, B_IN, 0, 416, BANK, 6, rm)
                sp.wait_ge(s.final_done, 2)
                broadcast(gain_m[:, :], "mix_norm_2", l * D, D, s.gain_m_landed)
                block_units("w_in_2", l, B_IN, 0, 928, BANK, 8, rm)
                load(10 % SLOTS, rm + 3, [
                    (raw[0:PC, 1, u * 2 * PC:(u + 1) * 2 * PC].rearrange("p (g n) -> p g n", g=2),
                     dram("pool_w_2", l * (4 * PC * PC) + u * 2 * PC * PC, (PC, PC), (PC * PC, 2), (1, PC))) for u in range(2)])
                for n in range(2):
                    block_units("w_o_2", l, D, 0, n * BANK, BANK, 11 + 2 * n, rm)
                rf, _, _, _ = ffn_stage_b(l)
                ffn("w_gate_up_2", "w_down_2", l, rf)

            sp.wait_ge(s.xn_ready, 8 * DEPTH + 6 * DEPTH + 1)
            broadcast(gain_m[:, :], "final_norm_2", 0, D, s.gain_m_landed)
            last_round = B_START + DEPTH * B_ROUNDS - 1
            for slot in range(2):
                sp.wait_ge(s.w_lo_ready, unit(slot, last_round) + 4)
                sp.sem_inc(raw_landed[slot], 32)
            for t in range(TT):
                sp.wait_ge(s.final_done, 2 + t + 1)
                sp.dma_start(out[0, tok(t), :], xn[:, t, :]).then_inc(s.out_stored, 16)
            sp.wait_ge(s.out_stored, 16 * TT)

        @block.gpsimd
        def _(pool):
            pool.memset(ident[:, :], 0.0).then_inc(s.ident_zero, 1)
            pool.memset(eps[:, :], EPS)
            pool.memset(neghalf[:, :], -0.5).then_inc(s.half_ready, 1)
            pool.wait_ge(s.ident_zero, 1)
            pool.affine_select(out=ident[:, :], in_=ident[:, :], compare_op=ALU.not_equal, fill=1.0, base=0,
                               pattern=[[-1, P]], channel_multiplier=1).then_inc(s.ident_ready, 1)
            pool.wait_ge(s.half_ready, 1)

            def rsqrt(mean, sums, result, n, ready, ms_sem, out_sem, count):
                pool.wait_ge(ready, count)
                pool.tensor_tensor(sums, mean, eps[:, 0:n], ALU.add).then_inc(ms_sem, 1)
                pool.wait_ge(ms_sem, count)
                pool.tensor_tensor(result, sums, neghalf[:, 0:n], ALU.pow).then_inc(out_sem, 1)

            def norm(n):
                for t in range(TT):
                    rsqrt(ss[:, t:t + 1], ms[:, t:t + 1], rstd[:, t:t + 1], 1, s.sq_ready, s.ms_ready, s.rstd_ready,
                          2 * n + t + 1)

            with pool.Fori(0, DEPTH) as l:
                norm(3 * l)
                pool.wait_ge(s.bias_landed, 64 * l + 64)
                pool.wait_ge(s.consts_a_landed, 16 * l + 16)
                flat = bias.rearrange("p t h k -> p (t h) k")
                pool.tensor_tensor(flat, flat, consts_a[:, CA_MASK:].unsqueeze(1).to_broadcast([P, TT * NA_H, T]),
                                   ALU.add).then_inc(s.bias_masked, 1)
                norm(3 * l + 1)
                norm(3 * l + 2)
            norm(6)
            with pool.Fori(0, DEPTH) as l:
                norm(7 + 2 * l)
                for t in range(TT):
                    rsqrt(c_ss[:, t, :], c_m[:, t, :], c_r[:, t, :], 2, s.c_sq, s.c_ms, s.c_rstd, 2 * l + t + 1)
                pool.wait_ge(s.consts_b_landed, 16)
                for t in range(TT):
                    kr = c_nat[:, t, QR + KVR:C_COLS]
                    h = ROPE // 2
                    pool.tensor_tensor(krA[:, t, :], kr, rope_table(t, 0), ALU.mult)
                    pool.tensor_tensor(krB[:, t, 0:h], kr[:, h:], rope_table(t, 1)[:, 0:h], ALU.mult)
                    pool.tensor_tensor(krB[:, t, h:], kr[:, 0:h], rope_table(t, 1)[:, h:], ALU.mult).then_inc(s.krot_a, 1)
                    pool.wait_ge(s.krot_a, 2 * l + t + 1)
                    dst = mk[:, t, :].rearrange("p (h c) -> p h c", h=MLA_H)[:, :, NOPE:]
                    pool.tensor_tensor(dst, krA[:, t, :].unsqueeze(1).to_broadcast([P, MLA_H, ROPE]),
                                       krB[:, t, :].unsqueeze(1).to_broadcast([P, MLA_H, ROPE]), ALU.add).then_inc(s.krot_ready, 1)
                pool.wait_ge(s.small_landed, 80 * l + 80)
                for t in range(TT):
                    pool.wait_ge(s.z_ready, 2 * l + t + 1)
                    taps = small[:, convw_at:convw_at + CONV_W * GD].rearrange("p (i c) -> p i c", i=CONV_W)
                    pool.tensor_tensor(zw[:, t, :, :], z[:, t, :].unsqueeze(1).to_broadcast([P, CONV_W, GD]), taps,
                                       ALU.mult).then_inc(s.zw_ready, 1)
                for t in range(TT):
                    rsqrt(g_ss[:, t, :], g_m[:, t, :], g_r[:, t, :], 4, s.gsq_ready, s.gms_ready, s.grstd_ready,
                          2 * l + t + 1)
                norm(7 + 2 * l + 1)
            norm(11)

        @block.scalar
        def _(act_e):
            rpb = a["na_rpb"].tensor
            with nc.allow_non_contiguous_dma(reason="rows of 64 keys"):
                for l in range(DEPTH):
                    for dr in range(NA_DR):
                        row = (l * NA_H * RPB_R + (dr + 8 - GRID_H)) * RPB_C + RPB_C // 2
                        src = bass.AP(tensor=rpb, offset=row, ap=[[RPB_R * RPB_C, NA_H], [-1, GRID_W], [1, GRID_W]])
                        act_e.dma_start(spread[l, :, :, dr * GRID_W:(dr + 1) * GRID_W].rearrange("q h k -> h q k"), src).then_inc(s.rpb_spread, 16)

            def refill(slot, rnd):
                u = unit(slot, rnd)
                act_e.wait_ge(s.unit_done, u + 1)
                act_e.wait_ge(raw_landed[slot], 32 * (rnd + 1))
                act_e.activation(whi[:, slot, :], raw[:, slot, :], ACT.Copy).then_inc(s.w_hi_ready, 1)

            def squares(n, r):
                for t in range(TT):
                    act_e.wait_ge(x_written[t], 2 * r + 1)
                    act_e.activation(xn[:, t, :], x[:, t, :], ACT.Square, scale=D ** -0.5,
                                 accum_out=ss[:, t:t + 1]).then_inc(s.sq_ready, 1)

            def transposed_hi(o):
                for t in range(TT):
                    for b in range(2):
                        act_e.wait_ge(s.tr_done, 4 * o + 2 * t + b + 1)
                        act_e.activation(xTh[:, 4 * b:4 * b + 4, tok(t)], pg[b][t][:, :].rearrange("p (c n) -> p c n", c=4),
                                         ACT.Copy).then_inc(s.xT_hi_ready, 1)

            def ffn(rnd, f, n, o):
                squares(n, n)
                refill(2, rnd)
                transposed_hi(o)

                def silu(t, par):
                    act_e.activation(sg[:, t, :], pg[par][t][:, 0:FB], ACT.Silu).then_inc(s.silu_ready, 1)

                act_e.wait_ge(s.ffn_t0_done, 12 * f + 1)
                silu(0, 0)
                refill(0, rnd + 1)
                act_e.wait_ge(s.unit_done, unit(1, rnd) + 4)
                silu(1, 0)
                refill(1, rnd + 1)

                def product_hi(j, par):
                    act_e.wait_ge(s.actT_tr, STEPS * f + j + 1)
                    act_e.activation(bTh[:, 0:2, :], pg[par][0][:, :].rearrange("p (c n) -> p c n", c=2),
                                     ACT.Copy).then_inc(s.actT_hi, 1)

                with act_e.Fori(0, (STEPS - 1) // 2) as jj:
                    for par in range(2):
                        j = 2 * jj + par
                        product_hi(j, par)
                        act_e.wait_ge(s.ffn_t0_done, 12 * f + j + 2)
                        silu(0, 1 - par)
                        refill(2, rnd + j + 1)
                        act_e.wait_ge(s.unit_done, unit(0, rnd + j + 1) + 4)
                        silu(1, 1 - par)
                        refill(0, rnd + j + 2)
                        refill(1, rnd + j + 2)
                product_hi(STEPS - 1, 0)

            def copy(dst, src, sem, scale=1.0):
                act_e.activation(dst, src, ACT.Copy, scale=scale).then_inc(sem, 1)

            def mixer_a(l):
                rnd, r, o = mixa_stage(l)
                squares(r, r)
                refill(2, rnd)
                transposed_hi(o)

                def refills(*units):
                    for i in units:
                        refill(i % SLOTS, rnd + i // SLOTS)

                def block_done(b, t):
                    if t == 0:
                        act_e.wait_ge(s.mixa_t0_done, 14 * l + b + 1)
                    else:
                        act_e.wait_ge(s.unit_done, unit(0, rnd) + 2 * b + 1 + 4)

                for b, (dst, sem, scale) in enumerate(((q_nat, s.qk_sb, NA_SCALE), (k_nat, s.qk_sb, 1.0), (v_nat, s.v_sb, 1.0))):
                    for t in range(TT):
                        block_done(b, t)
                        copy(dst[:, t, :], pg[b % 2][t][:, :], sem, scale)
                    refills(2 * b + 3, 2 * b + 4)

                def probs_T(i):
                    act_e.wait_ge(s.naPT_done, 8 * l + i + 1)
                    copy(probsT[:, i % 2, :], acc[2][:, :], s.naPT_sb)

                def sigmoid(g, t):
                    act_e.wait_ge(s.gate_added, 8 * l + 2 * g + t + 1)
                    part = gate[:, t, g * BANK:(g + 1) * BANK]
                    act_e.activation(part, part, ACT.Sigmoid).then_inc(s.gate_sig, 1)

                for i in range(10):
                    if i < 2:
                        block_done(3, i)
                        copy(uf[:, i, :], pg[1][i][:, :], s.uf_sb)
                    if 1 <= i <= 8:
                        probs_T(i - 1)
                    if i < 8:
                        act_e.wait_ge(s.na_negmax, 8 * l + i + 1)
                        t, hp = i // 4, i % 4
                        for e in range(2):
                            h = 4 * (hp // 2) + hp % 2 + 2 * e
                            part = probs[:, i % 2, e * T:(e + 1) * T]
                            last = act_e.activation(part, part, ACT.Exp, bias=na_neg[:, i, e:e + 1],
                                                    accum_out=na_sum[:, t, h:h + 1])
                        last.then_inc(s.na_exp, 1)
                    if i >= 2:
                        g = (i - 2) // 2
                        if i % 2 == 0:
                            act_e.wait_ge(s.dft1_done, 4 * l + g + 1)
                            copy(dft, acc[1][:, :], s.dft1_sb)
                        else:
                            act_e.wait_ge(s.dft2_done, 4 * l + g + 1)
                            copy(fTh[:, g, :], acc[1][:, 0:T], s.fT_hi)
                    if i % 2 == 1:
                        b = 3 + i // 2
                        refills(2 * b + 3, 2 * b + 4)
                    if i == 8:
                        for g in range(3):
                            for t in range(TT):
                                sigmoid(g, t)
                for t in range(TT):
                    sigmoid(3, t)
                refills(19)
                for t in range(TT):
                    act_e.wait_ge(s.oT_tr, 2 * l + t + 1)
                    copy(oTh[:, :, tok(t)], acc[2 * t][:, :].rearrange("p (c n) -> p c n", c=4), s.oT_hi)
                refills(20, 21, 22)
                transposed_hi(o + 1)
                refills(23, 24, 25)

            def mixer_b(l):
                rnd, r, o = mixb_stage(l)
                squares(r, r)
                refill(2, rnd)
                transposed_hi(o)

                def refills(*units):
                    for i in units:
                        refill(i % SLOTS, rnd + i // SLOTS)

                def done(b, i, t):
                    if t == 0:
                        act_e.wait_ge(s.mixb_t0_done, 8 * l + b + 1)
                    else:
                        act_e.wait_ge(s.unit_done, unit(0, rnd) + i + 4)

                for t in range(TT):
                    done(0, 1, t)
                    copy(c_nat[:, t, :], pg[0][t][:, 0:C_COLS], s.c_sb)
                    act_e.wait_ge(s.c_sb, 2 * l + t + 1)
                    act_e.activation(xn[:, t, 0:QR], c_nat[:, t, 0:QR], ACT.Square, scale=QR ** -0.5, accum_out=c_ss[:, t, 0:1])
                    act_e.activation(xn[:, t, QR:QR + KVR], c_nat[:, t, QR:QR + KVR], ACT.Square, scale=KVR ** -0.5,
                                     accum_out=c_ss[:, t, 1:2]).then_inc(s.c_sq, 1)
                refills(3, 4)
                for t in range(TT):
                    done(1, 3, t)
                    copy(sw_nat[:, t, :], pg[1][t][:, :], s.sw_sb)
                refills(5, 6)
                for t in range(TT):
                    act_e.wait_ge(s.cT_tr, 2 * l + t + 1)
                    copy(cTh[:, :, tok(t)], acc[t][:, 0:3 * P].rearrange("p (c n) -> p c n", c=3), s.cT_hi)
                for t in range(TT):
                    done(3, 5, t)
                    heads = acc[2 + t][:, :].rearrange("p (h c) -> p h c", h=MLA_H)
                    act_e.activation(mk[:, t, :].rearrange("p (h c) -> p h c", h=MLA_H)[:, :, 0:NOPE], heads[:, :, 0:NOPE], ACT.Copy)
                    copy(mv[:, t, :].rearrange("p (h c) -> p h c", h=MLA_H), heads[:, :, NOPE:], s.knope_sb)
                refills(7, 8)

                def sw_exp(i):
                    n, keys, h0, t = units_b[i]
                    act_e.wait_ge(s.sw_sinkarg, 3 * l + i + 1)
                    for e in range(n):
                        part = sP[:, e * keys:(e + 1) * keys]
                        last = act_e.activation(part, part, ACT.Exp, bias=s_neg[:, i, e:e + 1],
                                                accum_out=s_sum[:, t, h0 + e:h0 + e + 1])
                    last.then_inc(s.sw_exp, 1)
                    act_e.activation(s_snk[:, i, 0:n], s_arg[:, i, 0:n], ACT.Exp).then_inc(s.sw_sinkexp, 1)

                def mla_exp(i):
                    n, keys, h0, t = units_b[i]
                    act_e.wait_ge(s.mla_negmax, 3 * l + i + 1)
                    for e in range(n):
                        part = mP[:, e * keys:(e + 1) * keys]
                        last = act_e.activation(part, part, ACT.Exp, bias=m_neg[:, i, e:e + 1],
                                                accum_out=m_sum[:, t, h0 + e:h0 + e + 1])
                    last.then_inc(s.mla_exp, 1)

                def sw_probs_T(i):
                    act_e.wait_ge(s.swPT_done, 3 * l + i + 1)
                    copy(sPT, acc[2][:, :], s.swPT_sb)

                def mla_probs_T(i):
                    act_e.wait_ge(s.mlaPT_done, 3 * l + i + 1)
                    copy(mPT, acc[2][:, :], s.mlaPT_sb)

                def gates_copy(t):
                    done(4, 7, t)
                    copy(gates[:, t, :], pg[0][t][:, :], s.gates_sb)

                sw_exp(0)
                gates_copy(0)
                for t, bank in ((0, 3), (1, 1)):
                    act_e.wait_ge(s.mlaT_tr, 4 * l + 3 + t)
                    copy(mkT[0:MLA_D, :, tok(t)], acc[bank][0:MLA_D, :].rearrange("p (h n) -> p h n", h=MLA_H), s.mlaT_k_sb)
                sw_probs_T(0)
                sw_exp(1)
                gates_copy(1)
                refills(9, 10)
                mla_exp(0)
                sw_probs_T(1)
                sw_exp(2)
                mla_probs_T(0)
                mla_exp(1)
                sw_probs_T(2)
                refills(11, 12)
                mla_probs_T(1)
                mla_exp(2)
                mla_probs_T(2)
                act_e.wait_ge(s.pooled_done, l + 1)
                for b in range(2):
                    last = act_e.activation(plTh[0:PC, 2 * b:2 * b + 2, :], pg[1][b][0:PC, :].rearrange("p (g n) -> p g n", g=2), ACT.Copy)
                last.then_inc(s.pooled_hi, 1)
                refills(13)
                act_e.wait_ge(s.conv_sb, l + 1)
                act_e.wait_ge(s.pool_sb, l + 1)
                act_e.wait_ge(s.sw_o_sb, 2 * l + 2)
                for t in range(TT):
                    act_e.wait_ge(s.mla_o_sb, 2 * l + t + 1)
                    for g in range(4):
                        last = act_e.activation(unused[t][:, g, :], y[:, t, g * GD:(g + 1) * GD], ACT.Square, scale=GD ** -0.5,
                                                accum_out=g_ss[:, t, g:g + 1])
                    last.then_inc(s.gsq_ready, 1)
                transposed_hi(o + 1)
                refills(14, 15, 16)

            refill(0, 0)
            refill(1, 0)
            with act_e.Fori(0, DEPTH) as l:
                for m, (rnd, f, n, o) in enumerate(ffn_stages_a(l)):
                    ffn(rnd, f, n, o)
                    if m == 0:
                        mixer_a(l)
            squares(6, 6)
            with act_e.Fori(0, DEPTH) as l:
                mixer_b(l)
                rnd, f, n, o = ffn_stage_b(l)
                ffn(rnd, f, n, o)
            squares(11, 11)

        @block.vector
        def _(v):
            def refill(slot, rnd):
                v.wait_ge(s.w_hi_ready, unit(slot, rnd) + 1)
                v.tensor_tensor(wlo[:, slot, :], raw[:, slot, :], f32(whi[:, slot, :]), ALU.subtract).then_inc(s.w_lo_ready, 1)

            def scale(n, o, gain, landed, count):
                v.wait_ge(landed, count)
                for t in range(TT):
                    v.wait_ge(s.rstd_ready, 2 * n + t + 1)
                    v.scalar_tensor_tensor(xn[:, t, :], x[:, t, :], rstd[:, t:t + 1], gain[:, :], ALU.mult, ALU.mult)\
                        .then_inc(s.xn_ready, 1)

            def transposed_lo(o):
                for t in range(TT):
                    for b in range(2):
                        v.wait_ge(s.xT_hi_ready, 4 * o + 2 * t + b + 1)
                        part = slice(4 * b, 4 * b + 4)
                        v.tensor_tensor(xTl[:, part, tok(t)], pg[b][t][:, :].rearrange("p (c n) -> p c n", c=4),
                                        f32(xTh[:, part, tok(t)]), ALU.subtract).then_inc(s.xT_lo_ready, 1)

            def residual(t, n, bank, factor):
                part = x[:, t, n * BANK:(n + 1) * BANK]
                v.scalar_tensor_tensor(part, bank[:, :], factor, part, ALU.mult, ALU.add).then_inc(x_written[t], 1)

            def ffn(rnd, f, n, o, gain, landed, count, factor):
                scale(n, o, gain, landed, count)
                refill(2, rnd)
                transposed_lo(o)

                def product(t, par, j):
                    v.wait_ge(s.silu_ready, 2 * STEPS * f + 2 * j + t + 1)
                    v.tensor_tensor(act[:, t, :], sg[:, t, :], pg[par][t][:, FB:2 * FB], ALU.mult).then_inc(s.act_ready, 1)

                product(0, 0, 0)
                refill(0, rnd + 1)
                product(1, 0, 0)
                refill(1, rnd + 1)

                def product_lo(j, par):
                    v.wait_ge(s.actT_hi, STEPS * f + j + 1)
                    v.tensor_tensor(bTl[:, 0:2, :], pg[par][0][:, :].rearrange("p (c n) -> p c n", c=2),
                                    f32(bTh[:, 0:2, :]), ALU.subtract).then_inc(s.actT_lo, 1)

                with v.Fori(0, (STEPS - 1) // 2) as jj:
                    for par in range(2):
                        j = 2 * jj + par
                        product_lo(j, par)
                        product(0, 1 - par, j + 1)
                        refill(2, rnd + j + 1)
                        product(1, 1 - par, j + 1)
                        refill(0, rnd + j + 2)
                        refill(1, rnd + j + 2)
                product_lo(STEPS - 1, 0)
                v.wait_ge(s.ffn_t0_done, 12 * f + 12)
                for n2 in range(2):
                    residual(0, n2, acc[n2], factor)
                v.wait_ge(s.unit_done, unit(2, rnd + STEPS - 1) + 4)
                for n2 in range(2):
                    residual(1, n2, acc[2 + n2], factor)

            def mixer_a(l):
                rnd, r, o = mixa_stage(l)
                scale(r, o, gain_m, s.gain_m_landed, 16 * l + 16)
                refill(2, rnd)
                transposed_lo(o)

                def refills(*units):
                    for i in units:
                        refill(i % SLOTS, rnd + i // SLOTS)

                def done(b, i, t):
                    if t == 0:
                        v.wait_ge(s.mixa_t0_done, 14 * l + b + 1)
                    else:
                        v.wait_ge(s.unit_done, unit(0, rnd) + i + 4)

                refills(3, 4, 5, 6)

                def heads_T(n, dst, t, bank):
                    v.wait_ge(s.qkT_tr, 4 * l + n + 1)
                    v.tensor_copy(dst[:, :, tok(t)], bank[:, :].rearrange("p (c n) -> p c n", c=4)).then_inc(s.qkT_sb, 1)

                for n, dst in enumerate((qT, kT)):
                    for t in range(TT):
                        heads_T(2 * n + t, dst, t, acc[2 * n + t])
                refills(7, 8)
                v.wait_ge(s.bias_masked, l + 1)
                v.wait_ge(s.gate_bias_landed, 32 * l + 32)

                def add_gate_bias(g, t):
                    done(4 + g, 2 * (4 + g) + 1, t)
                    part = gate[:, t, g * BANK:(g + 1) * BANK]
                    v.tensor_tensor(part, pg[g % 2][t][:, :], part, ALU.add).then_inc(s.gate_added, 1)

                def softmax_max(i):
                    t, hp = i // 4, i % 4
                    h = 4 * (hp // 2) + hp % 2
                    v.wait_ge(s.na_scores, 8 * l + i + 1)
                    p3 = probs[:, i % 2, :].rearrange("p (e k) -> p e k", e=2)
                    v.tensor_tensor(p3, acc[0][:, :].rearrange("p (e k) -> p e k", e=2), bias[:, t, h:h + 3:2, :],
                                    ALU.add).then_inc(s.na_biased, 1)
                    v.wait_ge(s.na_biased, 8 * l + i + 1)
                    v.tensor_reduce(na_neg[:, i, :], p3, AX.X, ALU.max, negate=True).then_inc(s.na_negmax, 1)

                def normalise(t):
                    v.wait_ge(s.na_exp, 8 * l + 4 * t + 4)
                    v.reciprocal(na_inv[:, t, :], na_sum[:, t, :]).then_inc(s.na_rinv, 1)
                    v.wait_ge(s.na_rinv, 2 * l + t + 1)
                    v.wait_ge(s.na_o_done, 8 * l + 4 * t + 4)
                    v.tensor_tensor(o_nat[:, t, :].rearrange("p (h c) -> p h c", h=NA_H),
                                    acc[3][:, :].rearrange("p (h c) -> p h c", h=NA_H),
                                    na_inv[:, t, :].unsqueeze(2).to_broadcast([P, NA_H, NA_D]), ALU.mult).then_inc(s.na_o_sb, 1)

                for i in range(10):
                    if i >= 2:
                        add_gate_bias((i - 2) // 2, i % 2)
                    if i == 6:
                        normalise(0)
                    if i < 8:
                        softmax_max(i)
                    if i >= 2 and i % 2 == 1:
                        g = (i - 2) // 2
                        v.wait_ge(s.fT_hi, 4 * l + g + 1)
                        v.tensor_tensor(fTl[:, g, :], acc[1][:, 0:T], f32(fTh[:, g, :]), ALU.subtract).then_inc(s.fT_lo, 1)
                    if i % 2 == 1:
                        b = 3 + i // 2
                        refills(2 * b + 3, 2 * b + 4)

                def mixed(n, t, g, bank):
                    return gate[:, t, g * D + n * BANK:g * D + (n + 1) * BANK]

                def from_fourier(n, t):
                    done(8 + n, 16 + n, t)
                    v.wait_ge(s.gate_sig, 8 * l + 8)
                    v.tensor_tensor(xn[:, t, n * BANK:(n + 1) * BANK], pg[n][t][:, :], mixed(n, t, 1, None), ALU.mult)\
                        .then_inc(s.mix_f_ready, 1)

                def from_attention(n, t):
                    done(10 + n, 18 + n, t)
                    part = mixed(n, t, 0, None)
                    v.tensor_tensor(part, acc[(1, 3, 0, 2)[2 * n + t]][:, :], part, ALU.mult).then_inc(s.mix_na_ready, 1)
                    v.wait_ge(s.mix_na_ready, 4 * l + 2 * n + t + 1)
                    v.wait_ge(s.mix_f_ready, 4 * l + 4)
                    full = xn[:, t, n * BANK:(n + 1) * BANK]
                    add = v.tensor_tensor(full, full, part, ALU.add)
                    if n == 1:
                        add.then_inc(s.xn_ready, 1)

                normalise(1)
                from_fourier(0, 0)
                from_fourier(0, 1)
                refills(19)
                for t in range(TT):
                    v.wait_ge(s.oT_hi, 2 * l + t + 1)
                    v.tensor_tensor(oTl[:, :, tok(t)], acc[2 * t][:, :].rearrange("p (c n) -> p c n", c=4),
                                    f32(oTh[:, :, tok(t)]), ALU.subtract).then_inc(s.oT_lo, 1)
                from_fourier(1, 0)
                from_fourier(1, 1)
                refills(20)
                from_attention(0, 0)
                from_attention(0, 1)
                refills(21)
                from_attention(1, 0)
                from_attention(1, 1)
                refills(22)
                transposed_lo(o + 1)
                done(12, 21, 0)
                residual(0, 0, acc[0], 1.0)
                done(12, 21, 1)
                residual(1, 0, acc[2], 1.0)
                refills(23, 24)
                done(13, 23, 0)
                residual(0, 1, acc[1], 1.0)
                refills(25)
                done(13, 23, 1)
                residual(1, 1, acc[3], 1.0)

            def mixer_b(l):
                rnd, r, o = mixb_stage(l)
                scale(r, o, gain_a, s.gain_a_landed, 16 * (DEPTH + l) + 16)
                refill(2, rnd)
                transposed_lo(o)

                def refills(*units):
                    for i in units:
                        refill(i % SLOTS, rnd + i // SLOTS)

                def done(b, i, t):
                    if t == 0:
                        v.wait_ge(s.mixb_t0_done, 8 * l + b + 1)
                    else:
                        v.wait_ge(s.unit_done, unit(0, rnd) + i + 4)

                refills(3, 4)
                v.wait_ge(s.small_landed, 80 * l + 80)
                v.wait_ge(s.consts_b_landed, 16)
                for t in range(TT):
                    v.wait_ge(s.c_rstd, 2 * l + t + 1)
                    for i, (c0, c1) in enumerate(((0, QR), (QR, QR + KVR))):
                        last = v.scalar_tensor_tensor(c_nat[:, t, c0:c1], c_nat[:, t, c0:c1], c_r[:, t, i:i + 1], small[:, c0:c1],
                                                      ALU.mult, ALU.mult)
                    last.then_inc(s.cn_ready, 1)
                refills(5, 6)
                for t in range(TT):
                    v.wait_ge(s.cT_hi, 2 * l + t + 1)
                    v.tensor_tensor(cTl[:, :, tok(t)], acc[t][:, 0:3 * P].rearrange("p (c n) -> p c n", c=3),
                                    f32(cTh[:, :, tok(t)]), ALU.subtract).then_inc(s.cT_lo, 1)
                for t in range(TT):
                    v.wait_ge(s.swqT_tr, 2 * l + t + 1)
                    v.tensor_copy(sqT[0:SW_D, :, tok(t)], acc[2 + t][0:SW_D, :].rearrange("p (h n) -> p h n", h=SW_H)).then_inc(s.swqT_sb, 1)
                v.wait_ge(s.swkT_tr, l + 1)
                v.tensor_copy(skT[0:SW_D, :, :], pg[0][0][0:SW_D, :].rearrange("p (h n) -> p h n", h=SW_KV)).then_inc(s.swkT_sb, 1)
                for t in range(TT):
                    done(2, 4, t)
                    h2 = ROPE // 2
                    q4 = acc[t][:, 0:MLA_H * MLA_D].rearrange("p (h c) -> p h c", h=MLA_H)
                    dst = mq[:, t, :].rearrange("p (h c) -> p h c", h=MLA_H)
                    cos = rope_table(t, 0).unsqueeze(1).to_broadcast([P, MLA_H, ROPE])
                    sin = rope_table(t, 1).unsqueeze(1)
                    v.tensor_copy(dst[:, :, 0:NOPE], q4[:, :, 0:NOPE])
                    v.tensor_tensor(ropeA[:, t, :, :], q4[:, :, NOPE:], cos, ALU.mult)
                    v.tensor_tensor(ropeB[:, t, :, 0:h2], q4[:, :, NOPE + h2:], sin[:, :, 0:h2].to_broadcast([P, MLA_H, h2]), ALU.mult)
                    v.tensor_tensor(ropeB[:, t, :, h2:], q4[:, :, NOPE:NOPE + h2], sin[:, :, h2:].to_broadcast([P, MLA_H, h2]),
                                    ALU.mult).then_inc(s.rope_a, 1)
                    v.wait_ge(s.rope_a, 2 * l + t + 1)
                    v.tensor_tensor(dst[:, :, NOPE:], ropeA[:, t, :, :], ropeB[:, t, :, :], ALU.add).then_inc(s.q_sb, 1)
                refills(7, 8)

                def sw_max(i):
                    n, keys, h0, t = units_b[i]
                    v.wait_ge(s.sw_scores, 3 * l + i + 1)
                    v.scalar_tensor_tensor(sP, acc[1][:, :], SW_D ** -0.5, consts_b[:, CB_SWA + i * BANK:CB_SWA + (i + 1) * BANK],
                                           ALU.mult, ALU.add).then_inc(s.sw_biased, 1)
                    v.wait_ge(s.sw_biased, 3 * l + i + 1)
                    v.tensor_reduce(s_max[:, i, 0:n], sP.rearrange("p (e k) -> p e k", e=n), AX.X, ALU.max).then_inc(s.sw_max, 1)
                    v.wait_ge(s.sw_max, 3 * l + i + 1)
                    sinks = small[:, sink_at + h0:sink_at + h0 + n]
                    v.tensor_tensor(s_max[:, i, 0:n], s_max[:, i, 0:n], sinks, ALU.max).then_inc(s.sw_maxed, 1)
                    v.wait_ge(s.sw_maxed, 3 * l + i + 1)
                    v.tensor_scalar(s_neg[:, i, 0:n], s_max[:, i, 0:n], -1.0, None, ALU.mult)
                    v.tensor_tensor(s_arg[:, i, 0:n], sinks, s_max[:, i, 0:n], ALU.subtract).then_inc(s.sw_sinkarg, 1)

                def mla_max(i):
                    n, keys, h0, t = units_b[i]
                    v.wait_ge(s.mla_scores, 3 * l + i + 1)
                    mask = causal[:, P:] if keys == P else causal
                    p3 = mP.rearrange("p (e k) -> p e k", e=n)
                    v.scalar_tensor_tensor(p3, acc[0][:, :].rearrange("p (e k) -> p e k", e=n), MLA_D ** -0.5,
                                           mask.unsqueeze(1).to_broadcast([P, n, keys]), ALU.mult, ALU.add).then_inc(s.mla_biased, 1)
                    v.wait_ge(s.mla_biased, 3 * l + i + 1)
                    v.tensor_reduce(m_neg[:, i, 0:n], p3, AX.X, ALU.max, negate=True).then_inc(s.mla_negmax, 1)

                def sw_out(t):
                    for i in ((0,), (1, 2))[t]:
                        n, keys, h0, _ = units_b[i]
                        v.wait_ge(s.sw_sinkexp, 3 * l + i + 1)
                        last = v.tensor_tensor(s_den[:, t, h0:h0 + n], s_sum[:, t, h0:h0 + n], s_snk[:, i, 0:n], ALU.add)
                    last.then_inc(s.sw_den, 1)
                    v.wait_ge(s.sw_den, 2 * l + t + 1)
                    v.reciprocal(s_inv[:, t, :], s_den[:, t, :]).then_inc(s.sw_rinv, 1)
                    v.wait_ge(s.sw_rinv, 2 * l + t + 1)
                    v.wait_ge(s.sw_o_done, 3 * l + (1, 3)[t])
                    v.tensor_tensor(y[:, t, 3 * GD:].rearrange("p (h c) -> p h c", h=SW_H),
                                    pg[0][1][:, 0:GD].rearrange("p (h c) -> p h c", h=SW_H),
                                    s_inv[:, t, :].unsqueeze(2).to_broadcast([P, SW_H, SW_D]), ALU.mult).then_inc(s.sw_o_sb, 1)

                def mla_out(t):
                    v.wait_ge(s.mla_exp, 3 * l + (1, 3)[t])
                    v.reciprocal(m_inv[:, t, :], m_sum[:, t, :]).then_inc(s.mla_rinv, 1)
                    v.wait_ge(s.mla_rinv, 2 * l + t + 1)
                    v.wait_ge(s.mla_o_done, 3 * l + (1, 3)[t])
                    v.tensor_tensor(y[:, t, 0:GD].rearrange("p (h c) -> p h c", h=MLA_H),
                                    acc[3][:, 0:GD].rearrange("p (h c) -> p h c", h=MLA_H),
                                    m_inv[:, t, :].unsqueeze(2).to_broadcast([P, MLA_H, MLA_V]), ALU.mult).then_inc(s.mla_o_sb, 1)

                def conv_in(t):
                    done(5, 9, t)
                    v.wait_ge(s.gates_sb, 2 * l + t + 1)
                    v.tensor_tensor(z[:, t, :], pg[1][t][:, 0:GD], gates[:, t, GD:], ALU.mult).then_inc(s.z_ready, 1)
                    v.tensor_copy(up[:, t, :], pg[1][t][:, GD:]).then_inc(s.up_sb, 1)

                sw_max(0)
                for t, bank in ((0, 0), (1, 2)):
                    v.wait_ge(s.mlaT_tr, 4 * l + t + 1)
                    v.tensor_copy(mqT[0:MLA_D, :, tok(t)], acc[bank][0:MLA_D, :].rearrange("p (h n) -> p h n", h=MLA_H)).then_inc(s.mlaT_q_sb, 1)
                sw_max(1)
                refills(9, 10)
                mla_max(0)
                sw_max(2)
                conv_in(0)
                sw_out(0)
                mla_max(1)
                conv_in(1)
                refills(11, 12)
                mla_out(0)
                mla_max(2)
                sw_out(1)
                v.wait_ge(s.conv_done, l + 1)
                v.tensor_tensor(y[:, :, GD:2 * GD], pg[0][0][:, :].rearrange("p (t c) -> p t c", t=TT), gates[:, :, 0:GD],
                                ALU.mult).then_inc(s.conv_sb, 1)
                v.wait_ge(s.pooled_hi, l + 1)
                for b in range(2):
                    part = slice(2 * b, 2 * b + 2)
                    last = v.tensor_tensor(plTl[0:PC, part, :], pg[1][b][0:PC, :].rearrange("p (g n) -> p g n", g=2),
                                           f32(plTh[0:PC, part, :]), ALU.subtract)
                last.then_inc(s.pooled_lo, 1)
                mla_out(1)
                v.wait_ge(s.unit_done, unit(0, rnd) + 10 + 4)
                v.tensor_tensor(y[:, :, 2 * GD:3 * GD], acc[1][:, :].rearrange("p (t c) -> p t c", t=TT),
                                small[:, pscale_at:pscale_at + GD].unsqueeze(1).to_broadcast([P, TT, GD]), ALU.mult).then_inc(s.pool_sb, 1)
                refills(13)
                v.wait_ge(s.gain_m_landed, 16 * (DEPTH + 1) + 16 * l + 16)
                for t in range(TT):
                    v.wait_ge(s.grstd_ready, 2 * l + t + 1)
                    for g in range(4):
                        c = slice(g * GD, (g + 1) * GD)
                        last = v.scalar_tensor_tensor(xn[:, t, c], y[:, t, c], g_r[:, t, g:g + 1], gain_m[:, c], ALU.mult, ALU.mult)
                    last.then_inc(s.xn_ready, 1)
                transposed_lo(o + 1)
                done(6, 12, 0)
                residual(0, 0, acc[0], 1.0)
                done(6, 12, 1)
                residual(1, 0, acc[2], 1.0)
                refills(14, 15)
                done(7, 14, 0)
                residual(0, 1, acc[1], 1.0)
                refills(16)
                done(7, 14, 1)
                residual(1, 1, acc[3], 1.0)

            def final(n, count, dst):
                v.wait_ge(s.gain_m_landed, count)
                for t in range(TT):
                    v.wait_ge(s.rstd_ready, 2 * n + t + 1)
                    ins = v.scalar_tensor_tensor(dst[:, t, :], x[:, t, :], rstd[:, t:t + 1], gain_m[:, :], ALU.mult, ALU.mult)
                    ins.then_inc(s.final_done, 1)
                    if dst is x:
                        v.wait_ge(s.final_done, t + 1)
                        for _ in range(2):
                            v.sem_inc(x_written[t], 1)

            v.sem_inc(s.w_lo_ready, SLOTS)
            v.sem_inc(s.xn_ready, 1)
            refill(0, 0)
            refill(1, 0)
            v.wait_ge(s.x_landed, 16)
            for t in range(TT):
                v.sem_inc(x_written[t], 1)
            with v.Fori(0, DEPTH) as l:
                (first, second) = ffn_stages_a(l)
                ffn(*first, gain_a, s.gain_a_landed, 16 * l + 16, 0.5)
                mixer_a(l)
                ffn(*second, gain_f, s.gain_f_landed, 16 * l + 16, 0.5)
            final(6, 16 * (DEPTH + 1), x)
            with v.Fori(0, DEPTH) as l:
                mixer_b(l)
                ffn(*ffn_stage_b(l), gain_f, s.gain_f_landed, 16 * (DEPTH + l) + 16, 1.0)
            final(11, 16 * (2 * DEPTH + 2), xn)

        @block.tensor
        def _(pe):
            def product(dst, pairs, first=True, last=True):
                for i, (xh, xl, wh, wl) in enumerate(pairs):
                    pe.matmul(dst, xh, wh, start=first and i == 0, stop=False)
                    pe.matmul(dst, xh, wl, start=False, stop=False)
                    mm = pe.matmul(dst, xl, wh, start=False, stop=last and i == len(pairs) - 1)
                return mm

            def weights(slot, at, n):
                return whi[:, slot, at:at + n], wlo[:, slot, at:at + n]

            def transposes(t, o):
                pe.wait_ge(s.xn_ready, 2 * o + t + 2)
                for c in range(KC):
                    tr = pe.transpose(pg[c // 4][t][:, (c % 4) * P:(c % 4 + 1) * P], xn[:, t, c * P:(c + 1) * P], ident[:, :])
                    if c % 4 == 3:
                        tr.then_inc(s.tr_done, 1)

            def operand_ready(t, o):
                pe.wait_ge(s.xT_lo_ready, 4 * o + 2 * t + 2)

            def split_ready(slot, rnd):
                pe.wait_ge(s.w_lo_ready, unit(slot, rnd) + 4)

            def half_block(t, half, slot, rnd, n, bank):
                if t == 0:
                    split_ready(slot, rnd)
                pairs = []
                for k in range(4):
                    c = 4 * half + k
                    pairs.append((xTh[:, c, tok(t)], xTl[:, c, tok(t)], *weights(slot, k * n, n)))
                return product(bank[:, 0:n], pairs, first=half == 0, last=half == 1)

            def full_block(slots, rnds, n, banks, t0_sem, between=None):
                for t in range(TT):
                    if t == 1 and between:
                        between()
                    for half in range(2):
                        mm = half_block(t, half, slots[half], rnds[half], n, banks[t])
                        if t == 1:
                            mm.then_inc(s.unit_done, 1)
                    if t == 0:
                        mm.then_inc(t0_sem, 1)

            def ffn(rnd, f, n, o):
                transposes(0, o)
                operand_ready(0, o)

                def second_tile():
                    transposes(1, o)
                    operand_ready(1, o)

                full_block((0, 1), (rnd, rnd), BANK, pg[0], s.ffn_t0_done, second_tile)

                def turn(j, par):
                    pe.wait_ge(s.act_ready, 2 * STEPS * f + 2 * j + 2)
                    for t in range(TT):
                        for c in range(2):
                            tr = pe.transpose(pg[par][0][:, c * T + t * P:c * T + (t + 1) * P], act[:, t, c * P:(c + 1) * P], ident[:, :])
                    tr.then_inc(s.actT_tr, 1)

                def down(j, slot, r, first, last):
                    pe.wait_ge(s.actT_lo, STEPS * f + j + 1)
                    split_ready(slot, r)
                    for t in range(TT):
                        for k in range(2):
                            for n2 in range(2):
                                mm = product(acc[2 * t + n2][:, :], [(bTh[:, k, tok(t)], bTl[:, k, tok(t)],
                                                                     *weights(slot, k * D + n2 * BANK, BANK))],
                                             first=first and k == 0, last=last and k == 1)
                        if last and t == 0:
                            mm.then_inc(s.ffn_t0_done, 1)
                    mm.then_inc(s.unit_done, 1)

                def step(j, par, first=False):
                    turn(j, par)
                    full_block((2, 0), (rnd + j, rnd + j + 1), BANK, pg[1 - par], s.ffn_t0_done)
                    down(j, 1, rnd + j + 1, first, False)

                step(0, 0, first=True)
                with pe.Fori(0, (STEPS - 3) // 2) as jj:
                    step(2 * jj + 1, 1)
                    step(2 * jj + 2, 0)
                step(STEPS - 2, 1)
                turn(STEPS - 1, 0)
                down(STEPS - 1, 2, rnd + STEPS - 1, False, True)

            def mixer_a(l):
                rnd, r, o = mixa_stage(l)

                def slots(i):
                    return ((i % SLOTS, (i + 1) % SLOTS), (rnd + i // SLOTS, rnd + (i + 1) // SLOTS))

                def in_block(b, between=None):
                    full_block(*slots(2 * b), BANK, pg[b % 2], s.mixa_t0_done, between)

                def second_tile():
                    transposes(1, o)
                    operand_ready(1, o)

                transposes(0, o)
                operand_ready(0, o)
                in_block(0, second_tile)
                in_block(1)

                def heads_T(src, n):
                    for t in range(TT):
                        pe.wait_ge(s.qk_sb, 4 * l + 2 * n + t + 1)
                        for c in range(4):
                            tr = pe.transpose(acc[2 * n + t][:, c * P:(c + 1) * P], src[:, t, c * P:(c + 1) * P], ident[:, :])
                        tr.then_inc(s.qkT_tr, 1)

                heads_T(q_nat, 0)
                in_block(2, lambda: heads_T(k_nat, 1))
                pe.wait_ge(s.v_sb, 2 * l + 2)
                pe.wait_ge(s.qkT_sb, 4 * l + 4)

                def scores(i):
                    t, hp = i // 4, i % 4
                    rows = slice(64 * (hp % 2), 64 * (hp % 2) + 64)
                    if i >= 1:
                        pe.wait_ge(s.na_biased, 8 * l + i)
                    for e in range(2):
                        c = 2 * (hp // 2) + e
                        mm = pe.matmul(acc[0][:, e * T:(e + 1) * T], qT[rows, c, tok(t)], kT[rows, c, :], start=True, stop=True)
                    mm.then_inc(s.na_scores, 1)

                def probs_T(i):
                    pe.wait_ge(s.na_exp, 8 * l + i + 1)
                    for e in range(2):
                        for kt in range(TT):
                            at = e * T + kt * P
                            tr = pe.transpose(acc[2][:, at:at + P], probs[:, i % 2, at:at + P], ident[:, :])
                    tr.then_inc(s.naPT_done, 1)

                def attend(i):
                    t, hp = i // 4, i % 4
                    pe.wait_ge(s.naPT_sb, 8 * l + i + 1)
                    if i == 4:
                        pe.wait_ge(s.na_o_sb, 2 * l + 1)
                    for e in range(2):
                        h = 4 * (hp // 2) + hp % 2 + 2 * e
                        for kt in range(TT):
                            at = e * T + kt * P
                            mm = pe.matmul(acc[3][:, h * NA_D:(h + 1) * NA_D], probsT[:, i % 2, at:at + P],
                                           v_nat[:, kt, h * NA_D:(h + 1) * NA_D], start=kt == 0, stop=kt == 1)
                    mm.then_inc(s.na_o_done, 1)

                def dft_positions(g):
                    if g == 0:
                        pe.wait_ge(s.uf_sb, 2 * l + 2)
                        pe.wait_ge(s.consts_a_landed, 16 * l + 16)
                    else:
                        pe.wait_ge(s.fT_lo, 4 * l + g)
                    for t in range(TT):
                        mm = pe.matmul(acc[1][:, :], uf[:, t, g * FC:(g + 1) * FC],
                                       consts_a[:, CA_DFT_T + t * 2 * T:CA_DFT_T + (t + 1) * 2 * T], start=t == 0, stop=t == 1)
                    mm.then_inc(s.dft1_done, 1)

                def dft_channels(g):
                    pe.wait_ge(s.dft1_sb, 4 * l + g + 1)
                    for n in range(2):
                        mm = pe.matmul(acc[1][:, 0:T], consts_a[:, CA_DFT_C + n * FC:CA_DFT_C + (n + 1) * FC],
                                       dft[:, n * T:(n + 1) * T], start=n == 0, stop=n == 1)
                    mm.then_inc(s.dft2_done, 1)

                for i in range(10):
                    b, t = 3 + i // 2, i % 2
                    sl, rn = slots(2 * b)
                    if b >= 6 and t == 0:
                        pe.wait_ge(s.gate_added, 8 * l + 2 * (b - 5))
                    if b == 5 and t == 0:
                        pe.wait_ge(s.uf_sb, 2 * l + 2)
                    for half in range(2):
                        mm = half_block(t, half, sl[half], rn[half], BANK, pg[b % 2][t])
                        if t == 1:
                            mm.then_inc(s.unit_done, 1)
                    if t == 0:
                        mm.then_inc(s.mixa_t0_done, 1)
                    if i < 8:
                        scores(i)
                    if 2 <= i:
                        attend(i - 2)
                    if 1 <= i <= 8:
                        probs_T(i - 1)
                    if i >= 2:
                        (dft_positions, dft_channels)[i % 2]((i - 2) // 2)

                def out_projection(i, idx, src_h, src_l, banks):
                    split_ready(i % SLOTS, rnd + i // SLOTS)
                    for t in range(TT):
                        mm = product(banks[t][:, :], [(src_h[:, k, tok(t)], src_l[:, k, tok(t)], *weights(i % SLOTS, k * BANK, BANK))
                                                      for k in range(4)])
                        mm.then_inc(s.mixa_t0_done if t == 0 else s.unit_done, 1)

                def attention_T(t):
                    pe.wait_ge(s.na_o_sb, 2 * l + t + 1)
                    for c in range(4):
                        tr = pe.transpose(acc[2 * t][:, c * P:(c + 1) * P], o_nat[:, t, c * P:(c + 1) * P], ident[:, :])
                    tr.then_inc(s.oT_tr, 1)

                pe.wait_ge(s.fT_lo, 4 * l + 4)
                pe.wait_ge(s.gate_added, 8 * l + 6)
                out_projection(16, 8, fTh, fTl, pg[0])
                attention_T(0)
                attention_T(1)
                pe.wait_ge(s.gate_added, 8 * l + 8)
                out_projection(17, 9, fTh, fTl, pg[1])
                pe.wait_ge(s.oT_lo, 2 * l + 2)
                out_projection(18, 10, oTh, oTl, (acc[1], acc[3]))
                out_projection(19, 11, oTh, oTl, (acc[0], acc[2]))

                def second_operand():
                    transposes(1, o + 1)
                    operand_ready(1, o + 1)

                transposes(0, o + 1)
                operand_ready(0, o + 1)
                full_block(*slots(20), BANK, (acc[0], acc[2]), s.mixa_t0_done, second_operand)
                full_block(*slots(22), BANK, (acc[1], acc[3]), s.mixa_t0_done)

            def mixer_b(l):
                rnd, r, o = mixb_stage(l)

                def slots(i):
                    return ((i % SLOTS, (i + 1) % SLOTS), (rnd + i // SLOTS, rnd + (i + 1) // SLOTS))

                def second_tile():
                    transposes(1, o)
                    operand_ready(1, o)

                transposes(0, o)
                operand_ready(0, o)
                full_block(*slots(0), C_COLS, pg[0], s.mixb_t0_done, second_tile)
                full_block(*slots(2), BANK, pg[1], s.mixb_t0_done)
                for t in range(TT):
                    if t == 1:
                        pe.wait_ge(s.sw_sb, 2 * l + 2)
                    pe.wait_ge(s.cn_ready, 2 * l + t + 1)
                    for c in range(3):
                        tr = pe.transpose(acc[t][:, c * P:(c + 1) * P], c_nat[:, t, c * P:(c + 1) * P], ident[:, :])
                    tr.then_inc(s.cT_tr, 1)
                for t in range(TT):
                    for h in range(SW_H):
                        tr = pe.transpose(acc[2 + t][0:SW_D, h * P:(h + 1) * P], sw_nat[:, t, h * SW_D:(h + 1) * SW_D], ident[:, :])
                    tr.then_inc(s.swqT_tr, 1)
                for t in range(TT):
                    for h in range(SW_KV):
                        at = SW_H * SW_D + h * SW_D
                        tr = pe.transpose(pg[0][0][0:SW_D, h * T + t * P:h * T + (t + 1) * P], sw_nat[:, t, at:at + SW_D], ident[:, :])
                tr.then_inc(s.swkT_tr, 1)
                pe.wait_ge(s.cT_lo, 2 * l + 2)
                split_ready(1, rnd + 1)
                nq = MLA_H * MLA_D
                for t in range(TT):
                    mm = product(acc[t][:, 0:nq], [(cTh[:, k, tok(t)], cTl[:, k, tok(t)], *weights(1, k * nq, nq)) for k in range(2)])
                    mm.then_inc(s.mixb_t0_done if t == 0 else s.unit_done, 1)
                split_ready(2, rnd + 1)
                pe.wait_ge(s.swqT_sb, 2 * l + 2)
                for t in range(TT):
                    mm = product(acc[2 + t][:, :], [(cTh[:, 2, tok(t)], cTl[:, 2, tok(t)], *weights(2, 0, BANK))])
                    mm.then_inc(s.mixb_t0_done if t == 0 else s.unit_done, 1)
                pe.wait_ge(s.swkT_sb, l + 1)

                def sw_scores(i):
                    n, keys, h0, t = units_b[i]
                    if i == 0:
                        pe.wait_ge(s.q_sb, 2 * l + 2)
                    if i == 1:
                        pe.wait_ge(s.mlaT_k_sb, 2 * l + 2)
                    if i == 2:
                        pe.wait_ge(s.sw_biased, 3 * l + 2)
                    for e in range(n):
                        mm = pe.matmul(acc[1][:, e * keys:(e + 1) * keys], sqT[0:SW_D, h0 + e, tok(t)],
                                       skT[0:SW_D, (h0 + e) // 2, 0:keys], start=True, stop=True)
                    mm.then_inc(s.sw_scores, 1)

                def mla_scores(i):
                    n, keys, h0, t = units_b[i]
                    if i == 0:
                        pe.wait_ge(s.mlaT_q_sb, 2 * l + 2)
                        pe.wait_ge(s.mlaT_k_sb, 2 * l + 2)
                    else:
                        pe.wait_ge(s.mla_biased, 3 * l + i)
                    for e in range(n):
                        mm = pe.matmul(acc[0][:, e * keys:(e + 1) * keys], mqT[0:MLA_D, h0 + e, tok(t)],
                                       mkT[0:MLA_D, h0 + e, 0:keys], start=True, stop=True)
                    mm.then_inc(s.mla_scores, 1)

                def sw_probs_T(i):
                    pe.wait_ge(s.sw_exp, 3 * l + i + 1)
                    if i == 0:
                        pe.wait_ge(s.mlaT_q_sb, 2 * l + 2)
                    if i == 2:
                        pe.wait_ge(s.mlaPT_sb, 3 * l + 1)
                    for c in range(4):
                        tr = pe.transpose(acc[2][:, c * P:(c + 1) * P], sP[:, c * P:(c + 1) * P], ident[:, :])
                    tr.then_inc(s.swPT_done, 1)

                def mla_probs_T(i):
                    pe.wait_ge(s.mla_exp, 3 * l + i + 1)
                    if i < 2:
                        pe.wait_ge(s.swPT_sb, 3 * l + i + 2)
                    for c in range(4):
                        tr = pe.transpose(acc[2][:, c * P:(c + 1) * P], mP[:, c * P:(c + 1) * P], ident[:, :])
                    tr.then_inc(s.mlaPT_done, 1)

                def attend(i, bank, pT, value, sem):
                    n, keys, h0, t = units_b[i]
                    for e in range(n):
                        h = h0 + e
                        for kt in range(keys // P):
                            at = e * keys + kt * P
                            mm = pe.matmul(bank[:, h * 64:(h + 1) * 64], pT[:, at:at + P], value(kt, h), start=kt == 0, stop=kt == keys // P - 1)
                    mm.then_inc(sem, 1)

                def sw_attend(i):
                    pe.wait_ge(s.swPT_sb, 3 * l + i + 1)
                    if i == 0:
                        pe.wait_ge(s.gates_sb, 2 * l + 2)
                    if i == 1:
                        pe.wait_ge(s.sw_o_sb, 2 * l + 1)
                    at = (SW_H + SW_KV) * SW_D
                    attend(i, pg[0][1], sPT, lambda kt, h: sw_nat[:, kt, at + (h // 2) * SW_D:at + (h // 2 + 1) * SW_D], s.sw_o_done)

                def mla_attend(i):
                    pe.wait_ge(s.mlaPT_sb, 3 * l + i + 1)
                    if i == 1:
                        pe.wait_ge(s.mla_o_sb, 2 * l + 1)
                    attend(i, acc[3], mPT, lambda kt, h: mv[:, kt, h * MLA_V:(h + 1) * MLA_V], s.mla_o_done)

                def mla_heads_T():
                    for src, banks in ((mq, (0, 2)), (mk, (3, 1))):
                        for t in range(TT):
                            if src is mk and t == 0:
                                pe.wait_ge(s.krot_ready, 2 * l + 2)
                                pe.wait_ge(s.knope_sb, 2 * l + 2)
                            if banks[t] == 2:
                                pe.wait_ge(s.knope_sb, 2 * l + 2)
                            if banks[t] == 1:
                                pe.wait_ge(s.sw_biased, 3 * l + 1)
                            for h in range(MLA_H):
                                tr = pe.transpose(acc[banks[t]][0:MLA_D, h * P:(h + 1) * P], src[:, t, h * MLA_D:(h + 1) * MLA_D], ident[:, :])
                            tr.then_inc(s.mlaT_tr, 1)

                def conv():
                    pe.wait_ge(s.zw_ready, 2 * l + 2)

                    def shift(n):
                        return consts_b[:, CB_CONV + n * P:CB_CONV + (n + 1) * P]

                    for t in range(TT):
                        terms = [(shift(i), zw[:, t, i, :]) for i in range(CONV_W)]
                        if t == 1:
                            terms += [(shift(3 + i), zw[:, 0, i, :]) for i in range(2)]
                        for n, (m, taps) in enumerate(terms):
                            mm = pe.matmul(pg[0][0][:, t * GD:(t + 1) * GD], m, taps, start=n == 0, stop=n == len(terms) - 1)
                    mm.then_inc(s.conv_done, 1)

                def pooled():
                    pe.wait_ge(s.up_sb, 2 * l + 2)
                    for g in range(4):
                        dst = pg[1][g // 2][0:PC, (g % 2) * T:(g % 2 + 1) * T]
                        band = consts_b[:, CB_POOL + g * 3 * P:CB_POOL + (g + 1) * 3 * P]
                        chans = slice(g * PC, (g + 1) * PC)
                        pe.matmul(dst, up[:, 0, chans], band[:, 0:T], start=True, stop=False)
                        mm = pe.matmul(dst[:, P:T], up[:, 1, chans], band[:, T:], start=False, stop=True)
                    mm.then_inc(s.pooled_done, 1)

                def pool_mix():
                    pe.wait_ge(s.pooled_lo, l + 1)
                    split_ready(1, rnd + 3)
                    for t in range(TT):
                        for g in range(4):
                            mm = product(acc[1][:, t * GD + g * PC:t * GD + (g + 1) * PC],
                                         [(plTh[0:PC, g, tok(t)], plTl[0:PC, g, tok(t)],
                                           whi[0:PC, 1, g * PC:(g + 1) * PC], wlo[0:PC, 1, g * PC:(g + 1) * PC])])
                    mm.then_inc(s.unit_done, 1)

                for i in range(8):
                    b, t, half = 2 + i // 4, (i // 2) % 2, i % 2
                    u = 6 + 2 * (b - 2) + half
                    mm = half_block(t, half, u % SLOTS, rnd + u // SLOTS, BANK, pg[b % 2][t])
                    if t == 1:
                        mm.then_inc(s.unit_done, 1)
                    elif half == 1:
                        mm.then_inc(s.mixb_t0_done, 1)
                    if i == 1:
                        sw_scores(0)
                    if i == 2:
                        mla_heads_T()
                    if i == 3:
                        sw_probs_T(0)
                        sw_scores(1)
                    if i == 4:
                        mla_scores(0)
                    if i == 5:
                        sw_attend(0)
                        sw_probs_T(1)
                        sw_scores(2)
                    if i == 6:
                        mla_probs_T(0)
                        mla_scores(1)
                    if i == 7:
                        sw_attend(1)
                        sw_probs_T(2)
                mla_attend(0)
                mla_probs_T(1)
                mla_scores(2)
                sw_attend(2)
                conv()
                mla_attend(1)
                mla_probs_T(2)
                pooled()
                mla_attend(2)
                pool_mix()

                def second_operand():
                    transposes(1, o + 1)
                    operand_ready(1, o + 1)

                transposes(0, o + 1)
                operand_ready(0, o + 1)
                full_block(*slots(11), BANK, (acc[0], acc[2]), s.mixb_t0_done, second_operand)
                full_block(*slots(13), BANK, (acc[1], acc[3]), s.mixb_t0_done)

            pe.sem_inc(s.unit_done, SLOTS)
            pe.wait_ge(s.ident_ready, 1)
            with pe.Fori(0, DEPTH) as l:
                first, second = ffn_stages_a(l)
                ffn(*first)
                mixer_a(l)
                ffn(*second)
            with pe.Fori(0, DEPTH) as l:
                mixer_b(l)
                ffn(*ffn_stage_b(l))


INPUTS = """x ffn1_norm ffn1_w_in ffn1_w_out mix_norm mix_w_in mix_gate_bias na_rpb na_w_out f_w_out mix_w_o
ffn2_norm ffn2_w_in ffn2_w_out final_norm attn_norm_2 w_in_2 mla_q_norm_2 w_uq_2 mla_kv_norm_2 w_ukv_2 conv_w_2
pool_w_2 pool_scale_2 swa_sinks_2 mix_norm_2 w_o_2 ffn_norm_2 w_gate_up_2 w_down_2 final_norm_2""".split()


def kernel(**inputs):
    import concourse.bacc as bacc
    from concourse.bass_utils import run_bass_kernel_spmd

    nc = bacc.Bacc("TRN2", target_bir_lowering=False, num_devices=1)
    arrays = {n: np.ascontiguousarray(inputs[n]) for n in INPUTS}
    arrays["consts_a"] = first_constants()
    arrays["consts_b"] = second_constants()
    handles = {n: nc.dram_tensor(f"in_{n}", v.shape, F32, kind="ExternalInput").ap() for n, v in arrays.items()}
    out = nc.dram_tensor("out", (1, T, D), F32, kind="ExternalOutput").ap()
    build(nc, handles, out)
    r = run_bass_kernel_spmd(nc, [{f"in_{n}": v for n, v in arrays.items()}], core_ids=[0])
    return r.results[0]["out"]
```

```python
from contextlib import ExitStack

import numpy as np

import concourse.bass as bass
from concourse import mybir

F32 = mybir.dt.float32
F32R = mybir.dt.float32r
ACT = mybir.ActivationFunctionType
ALU = mybir.AluOpType
AX = mybir.AxisListType

P = 128
D = 1024
T = 256
TT = T // P
KC = D // P
DEPTH = 2
EPS = 1e-6
LOADED = 16
F = 2816
FB = 256
STEPS = F // FB
BANK = 512
UNIT = 4 * BANK
SLOTS = 3

GRID_W, NA_H, NA_D, NA_COLS = 64, 8, 64, 16
GRID_H = T // GRID_W
RPB_R, RPB_C = 15, 31
NA_SCALE = NA_D ** -0.5
NA_DR = 2 * GRID_H - 1
MASKED = -1e30
FG, FC = 4, 128
A_IN = 4096

MLA_H, NOPE, ROPE, MLA_V = 4, 64, 32, 64
MLA_D = NOPE + ROPE
QR, KVR = 256, 128
C_COLS = QR + KVR + ROPE
SW_H, SW_KV, SW_D = 4, 2, 64
WINDOWS = (2, 4, 8, 16)
PC = 64
CONV_W = 3
GD = 256
B_IN = 1952

FFN_ROUNDS = STEPS
MIXA_ROUNDS = 8
MIXB_ROUNDS = 5
A_ROUNDS = 2 * FFN_ROUNDS + MIXA_ROUNDS
B_ROUNDS = FFN_ROUNDS + MIXB_ROUNDS
B_START = DEPTH * A_ROUNDS

CA_DFT_T, CA_DFT_C, CA_MASK = 0, 2 * T, 2 * T + 2 * FC
CA_COLS = CA_MASK + T
CB_ROPE = 0
CB_CAUSAL = CB_ROPE + TT * 2 * ROPE
CB_SWA = CB_CAUSAL + T
CB_POOL = CB_SWA + 3 * BANK
CB_CONV = CB_POOL + len(WINDOWS) * 3 * P
CB_COLS = CB_CONV + 5 * P


def first_constants():
    out = np.zeros((P, CA_COLS), np.float32)
    norm = 1.0 / np.sqrt(T * FC)
    for odd in range(2):
        angle = 2 * np.pi * np.outer(np.arange(P), np.arange(odd, T, 2)) / T
        at = CA_DFT_T + odd * T
        out[:, at:at + T] = np.concatenate([np.cos(angle) * norm, np.sin(angle) * norm], 1)
    c = np.arange(FC)
    angle = 2 * np.pi * np.outer(c, c) / FC
    out[:, CA_DFT_C:CA_MASK] = np.concatenate([np.cos(angle), -np.sin(angle)], 1)
    col = np.arange(P) % GRID_W
    start = np.clip(col - NA_COLS // 2, 0, GRID_W - NA_COLS)[:, None]
    key = np.arange(T)[None, :] % GRID_W
    out[:, CA_MASK:] = np.where((key >= start) & (key < start + NA_COLS), 0.0, MASKED)
    return out


def second_constants():
    out = np.zeros((P, CB_COLS), np.float32)
    inv = (1.0 / (np.float32(10000.0) ** (np.arange(0, ROPE, 2, dtype=np.float32) / np.float32(ROPE))))
    ang = np.arange(T, dtype=np.float32)[:, None] * inv.astype(np.float32)[None, :]
    cos, sin = np.cos(ang), np.sin(ang)
    rope = np.concatenate([cos, cos, -sin, sin], 1)
    out[:, CB_ROPE:CB_CAUSAL] = rope.reshape(TT, P, 2 * ROPE).transpose(1, 0, 2).reshape(P, -1)
    q, k = np.arange(P)[:, None], np.arange(T)[None, :]
    out[:, CB_CAUSAL:CB_SWA] = np.where(k <= q + P, 0.0, MASKED)
    slopes = [2.0 ** (-8.0 * (h + 1) / SW_H) for h in range(SW_H)]
    dist = (q + P) - k
    for h in range(SW_H):
        near = (dist >= 0) & (dist < P)
        full = np.where(near, -slopes[h] * dist, MASKED)
        own = full[:, P:]
        out[:, CB_SWA + h * P:CB_SWA + (h + 1) * P] = own
        out[:, CB_SWA + BANK + h * T:CB_SWA + BANK + (h + 1) * T] = full
    s, t = np.arange(T)[:, None], np.arange(T)[None, :]
    for g, w in enumerate(WINDOWS):
        band = ((s <= t) & (s > t - w)) / np.minimum(t + 1, w) - (s == t)
        at = CB_POOL + g * 3 * P
        out[:, at:at + T] = band[:P]
        out[:, at + T:at + T + P] = band[P:, P:]
    s, t = np.arange(P)[:, None], np.arange(P)[None, :]
    for n, m in enumerate([t == s + 2, t == s + 1, t == s, t + P == s + 2, t + P == s + 1]):
        out[:, CB_CONV + n * P:CB_CONV + (n + 1) * P] = m
    return out


class Signals:

    def __init__(self, sem):
        self.consts_a_landed = sem("consts_a_landed")
        self.consts_b_landed = sem("consts_b_landed")
        self.rpb_spread = sem("rpb_spread")
        self.bias_landed = sem("bias_landed")
        self.gain_a_landed = sem("gain_a_landed")
        self.gain_m_landed = sem("gain_m_landed")
        self.gain_f_landed = sem("gain_f_landed")
        self.gate_bias_landed = sem("gate_bias_landed")
        self.small_landed = sem("small_landed")
        self.ident_zero = sem("ident_zero")
        self.ident_ready = sem("ident_ready")
        self.half_ready = sem("half_ready")
        self.bias_masked = sem("bias_masked")
        self.w_hi_ready = sem("w_hi_ready")
        self.w_lo_ready = sem("w_lo_ready")
        self.unit_done = sem("unit_done")
        self.x_written0 = sem("x_written0")
        self.x_written1 = sem("x_written1")
        self.sq_ready = sem("sq_ready")
        self.ms_ready = sem("ms_ready")
        self.rstd_ready = sem("rstd_ready")
        self.xn_ready0 = sem("xn_ready0")
        self.xn_ready1 = sem("xn_ready1")
        self.tr_done = sem("tr_done")
        self.xT_hi_ready = sem("xT_hi_ready")
        self.xT_lo_ready = sem("xT_lo_ready")
        self.ffn_t0_done = sem("ffn_t0_done")
        self.ffn_sum_done = sem("ffn_sum_done")
        self.silu_ready = sem("silu_ready")
        self.act_ready = sem("act_ready")
        self.actT_tr = sem("actT_tr")
        self.actT_hi = sem("actT_hi")
        self.actT_lo = sem("actT_lo")
        self.mixa_t0_done = sem("mixa_t0_done")
        self.qk_sb = sem("qk_sb")
        self.qkT_tr = sem("qkT_tr")
        self.qkT_sb = sem("qkT_sb")
        self.v_sb = sem("v_sb")
        self.uf_sb = sem("uf_sb")
        self.gate_added = sem("gate_added")
        self.gate_sig = sem("gate_sig")
        self.na_scores = sem("na_scores")
        self.na_biased = sem("na_biased")
        self.na_negmax = sem("na_negmax")
        self.na_exp = sem("na_exp")
        self.naPT_done = sem("naPT_done")
        self.naPT_sb = sem("naPT_sb")
        self.na_o_done = sem("na_o_done")
        self.na_rinv = sem("na_rinv")
        self.na_o_sb = sem("na_o_sb")
        self.oT_tr = sem("oT_tr")
        self.oT_hi = sem("oT_hi")
        self.oT_lo = sem("oT_lo")
        self.uf_diff = sem("uf_diff")
        self.uf_sum = sem("uf_sum")
        self.dft1_done = sem("dft1_done")
        self.dft1_sb = sem("dft1_sb")
        self.dft2_done = sem("dft2_done")
        self.fT_hi = sem("fT_hi")
        self.fT_lo = sem("fT_lo")
        self.mix_f_ready = sem("mix_f_ready")
        self.mix_na_ready = sem("mix_na_ready")
        self.mixb_t0_done = sem("mixb_t0_done")
        self.c_sb = sem("c_sb")
        self.c_sq = sem("c_sq")
        self.c_ms = sem("c_ms")
        self.c_rstd = sem("c_rstd")
        self.cn_ready = sem("cn_ready")
        self.cT_tr = sem("cT_tr")
        self.cT_hi = sem("cT_hi")
        self.cT_lo = sem("cT_lo")
        self.sw_sb = sem("sw_sb")
        self.swqT_tr = sem("swqT_tr")
        self.swqT_sb = sem("swqT_sb")
        self.swkT_tr = sem("swkT_tr")
        self.swkT_sb = sem("swkT_sb")
        self.rope_a = sem("rope_a")
        self.q_sb = sem("q_sb")
        self.krot_a = sem("krot_a")
        self.krot_ready = sem("krot_ready")
        self.knope_sb = sem("knope_sb")
        self.mlaT_tr = sem("mlaT_tr")
        self.mlaT_q_sb = sem("mlaT_q_sb")
        self.mlaT_k_sb = sem("mlaT_k_sb")
        self.sw_scores = sem("sw_scores")
        self.sw_biased = sem("sw_biased")
        self.sw_max = sem("sw_max")
        self.sw_maxed = sem("sw_maxed")
        self.sw_sinkarg = sem("sw_sinkarg")
        self.sw_exp = sem("sw_exp")
        self.sw_sinkexp = sem("sw_sinkexp")
        self.swPT_done = sem("swPT_done")
        self.swPT_sb = sem("swPT_sb")
        self.sw_o_done = sem("sw_o_done")
        self.sw_den = sem("sw_den")
        self.sw_rinv = sem("sw_rinv")
        self.sw_o_sb = sem("sw_o_sb")
        self.mla_scores = sem("mla_scores")
        self.mla_biased = sem("mla_biased")
        self.mla_negmax = sem("mla_negmax")
        self.mla_exp = sem("mla_exp")
        self.mlaPT_done = sem("mlaPT_done")
        self.mlaPT_sb = sem("mlaPT_sb")
        self.mla_o_done = sem("mla_o_done")
        self.mla_rinv = sem("mla_rinv")
        self.mla_o_sb = sem("mla_o_sb")
        self.in_sb = sem("in_sb")
        self.out_gate_sb = sem("out_gate_sb")
        self.z_ready = sem("z_ready")
        self.zw_ready = sem("zw_ready")
        self.conv_done = sem("conv_done")
        self.conv_sb = sem("conv_sb")
        self.pooled_done = sem("pooled_done")
        self.pooled_hi = sem("pooled_hi")
        self.pooled_lo = sem("pooled_lo")
        self.pool_sb = sem("pool_sb")
        self.gsq_ready = sem("gsq_ready")
        self.gms_ready = sem("gms_ready")
        self.grstd_ready = sem("grstd_ready")
        self.final_done = sem("final_done")
        self.out_stored = sem("out_stored")


def build(nc, a, out):
    with ExitStack() as ctx:
        def sb(name, shape, dt=F32):
            return ctx.enter_context(nc.sbuf_tensor(name, shape, dt))

        def psum(name):
            return ctx.enter_context(nc.psum_tensor(name, [P, BANK], F32))

        s = Signals(lambda name: ctx.enter_context(nc.semaphore(name)))
        raw_landed = [ctx.enter_context(nc.semaphore(f"raw_landed{i}")) for i in range(SLOTS)]
        x_written = [s.x_written0, s.x_written1]
        xn_ready = [s.xn_ready0, s.xn_ready1]

        raw = sb("raw", [P, SLOTS, UNIT])
        whi = sb("whi", [P, SLOTS, UNIT], F32R)
        wlo = sb("wlo", [P, SLOTS, UNIT], F32R)
        x = sb("x", [P, TT, D])
        xn = sb("xn", [P, TT, D])
        xTh = sb("xTh", [P, KC, T], F32R)
        xTl = sb("xTl", [P, KC, T], F32R)
        bTh = sb("bTh", [P, 8, T], F32R)
        bTl = sb("bTl", [P, 8, T], F32R)
        gain_a = sb("gain_a", [P, D])
        gain_m = sb("gain_m", [P, D])
        gain_f = sb("gain_f", [P, D])
        ident = sb("ident", [P, P])
        neghalf = sb("neghalf", [P, 8])
        eps = sb("eps", [P, 8])
        warm = sb("warm", [P, 1])
        ss = sb("ss", [P, TT])
        ms = sb("ms", [P, TT])
        rstd = sb("rstd", [P, TT])
        consts_a = sb("consts_a", [P, CA_COLS])
        shared = sb("shared", [P, TT * NA_H * T])
        bias = shared[:, :].rearrange("p (t h k) -> p t h k", t=TT, h=NA_H)
        consts_b = shared
        work = sb("work", [P, 13 * 1024])

        def area(at, *shape):
            n = int(np.prod(shape))
            v = work[:, at:at + n]
            if len(shape) == 2:
                v = v.rearrange("p (a b) -> p a b", a=shape[0])
            if len(shape) == 3:
                v = v.rearrange("p (a b c) -> p a b c", a=shape[0], b=shape[1])
            return v

        sg, act = area(12288, TT, FB), area(12800, TT, FB)
        squared = area(12288, D)

        gate = area(0, TT, 2 * D)
        q_nat, k_nat = area(4096, TT, BANK), area(5120, TT, BANK)
        o_nat = q_nat
        v_nat, uf = area(6144, TT, BANK), area(7168, TT, BANK)
        qT, kT = area(8192, 4, T), area(9216, 4, T)
        probs, probsT = area(10240, 2, BANK), area(11264, 2, BANK)
        dft = area(12288, BANK)
        uf_parts = uf[:, 0, :], area(12800, BANK)
        oTh, oTl, fTh, fTl = bTh[:, 0:4, :], bTl[:, 0:4, :], bTh[:, 4:8, :], bTl[:, 4:8, :]
        na_neg = sb("na_neg", [P, 8, 2])
        na_sum = sb("na_sum", [P, TT, NA_H])
        na_inv = sb("na_inv", [P, TT, NA_H])

        y = xn
        conv_pool_in, sw_nat = area(0, TT, BANK), area(1024, TT, BANK)
        c_nat = area(2048, TT, C_COLS)
        z = area(2048, TT, GD)
        small = area(2880, QR + KVR + CONV_W * GD + GD + SW_H)
        kvg_at, convw_at = QR, QR + KVR
        pscale_at = convw_at + CONV_W * GD
        sink_at = pscale_at + GD
        mqT, mkT = area(4352, MLA_H, T), area(5376, MLA_H, T)
        sqT = area(6400, SW_H, T)
        mP, mPT, sP, sPT = (area(7424 + i * BANK, BANK) for i in range(4))
        skT = area(9472, SW_KV, T)
        mq, mk = area(9984, TT, MLA_H * MLA_D), area(10752, TT, MLA_H * MLA_D)
        zw = area(9984, TT, CONV_W, GD)
        mv = area(11520, TT, MLA_H * MLA_V)
        ropeA, ropeB = area(12032, TT, MLA_H, ROPE), area(12288, TT, MLA_H, ROPE)
        group_squared = area(12032, 2, GD)
        krA, krB = area(12544, TT, ROPE), area(12608, TT, ROPE)
        out_gate = area(12672, TT, GD)
        cTh, cTl = bTh[:, 0:3, :], bTl[:, 0:3, :]
        plTh, plTl = bTh[:, 4:8, :], bTl[:, 4:8, :]
        c_ss, c_m, c_r = sb("c_ss", [P, TT, 2]), sb("c_m", [P, TT, 2]), sb("c_r", [P, TT, 2])
        m_neg, m_sum, m_inv = sb("m_neg", [P, 3, 4]), sb("m_sum", [P, TT, 4]), sb("m_inv", [P, TT, 4])
        s_max, s_neg, s_arg, s_snk = (sb(n, [P, 3, 4]) for n in ("s_max", "s_neg", "s_arg", "s_snk"))
        s_sum, s_den, s_inv = (sb(n, [P, TT, 4]) for n in ("s_sum", "s_den", "s_inv"))
        g_ss, g_m, g_r = (sb(n, [P, 2, TT * 2]) for n in ("g_ss", "g_m", "g_r"))

        pg = [[psum(f"pg{i}{t}") for t in range(TT)] for i in range(2)]
        acc = [psum(f"acc{i}") for i in range(4)]

        spread = nc.dram_tensor("rpb_spread", (GRID_W, DEPTH * NA_H, NA_DR * GRID_W), F32, kind="Internal").ap()

        causal = consts_b[:, CB_CAUSAL:CB_CAUSAL + T]

        def rope_table(t, which):
            at = CB_ROPE + (2 * t + which) * ROPE
            return consts_b[:, at:at + ROPE]

        def f32(ap):
            return ap.bitcast(F32)

        def tok(t):
            return slice(t * P, (t + 1) * P)

        def ffn_stages_a(l):
            return ((A_ROUNDS * l, 2 * l, 3 * l, 4 * l), (A_ROUNDS * l + FFN_ROUNDS + MIXA_ROUNDS, 2 * l + 1, 3 * l + 2, 4 * l + 3))

        def mixa_stage(l):
            return A_ROUNDS * l + FFN_ROUNDS, 3 * l + 1, 4 * l + 1

        def mixb_stage(l):
            return B_START + B_ROUNDS * l, 7 + 2 * l, 8 + 3 * l

        def ffn_stage_b(l):
            return B_START + B_ROUNDS * l + MIXB_ROUNDS, 4 + l, 7 + 2 * l + 1, 8 + 3 * l + 2

        pairs_b = ((2, 3), (0, 1))

        def pair_bank(t):
            return (acc[2], pg[1][0])[t]

        out_b = ((pg[0][0], acc[3]), (acc[1], acc[0]))

        units_b = ((4, P, 0, 0), (2, T, 0, 1), (2, T, 2, 1))

        def unit(slot, rnd):
            return SLOTS * rnd + slot

        block = ctx.enter_context(nc.Block())

        @block.sync
        def _(sp):
            def dram(t, offset, *dims):
                return bass.AP(tensor=a[t].tensor, offset=offset, ap=[list(d) for d in dims])

            def load(slot, rnd, pieces):
                sp.wait_ge(s.w_lo_ready, unit(slot, rnd) + 1)
                assert len(pieces) == 2
                for dst, src in pieces:
                    sp.dma_start(dst, src).then_inc(raw_landed[slot], 16)

            def rows(name, offset, pitch, slot, at, k, n):
                dst = raw[:, slot, at:at + k * n].rearrange("p (k n) -> p k n", k=k)
                return dst, dram(name, offset, (pitch, P), (pitch * P, k), (1, n))

            def broadcast(dst, name, offset, n, sem):
                sp.dma_start(dst, dram(name, offset, (0, P), (1, n))).then_inc(sem, 16)

            def block_units(name, l, pitch, width, col, n, first, rnd):
                for half in range(2):
                    i = first + half
                    at = l * (D * pitch) + half * (4 * P * pitch) + col
                    load(i % SLOTS, rnd + i // SLOTS,
                         [rows(name, at + 2 * u * P * pitch, pitch, i % SLOTS, 2 * u * n, 2, n) for u in range(2)])

            def ffn(w_in, w_out, l, rnd, breaks=((0, None),)):
                def gate_up(slots, rnds, j):
                    for half in range(2):
                        at = l * (D * 2 * F) + half * (4 * P * 2 * F) + j * FB
                        dst = raw[:, slots[half], :].rearrange("p (k n) -> p k n", k=4)
                        load(slots[half], rnds[half],
                             [(dst[:, :, u * FB:(u + 1) * FB], dram(w_in, at + u * F, (2 * F, P), (2 * F * P, 4), (1, FB)))
                              for u in range(2)])

                def down(slot, r, j):
                    at = l * (F * D) + j * (FB * D)
                    load(slot, r, [rows(w_out, at + k * P * D, D, slot, k * D, 1, D) for k in range(2)])

                gate_up((0, 1), (rnd, rnd), 0)
                for (begin, other), (end, _) in zip(breaks, (*breaks[1:], (STEPS - 1, None))):
                    if other:
                        other()
                    with sp.Fori(begin, end) as j:
                        gate_up((2, 0), (rnd + j, rnd + j + 1), j + 1)
                        down(1, rnd + j + 1, j)
                down(2, rnd + STEPS - 1, STEPS - 1)

            with sp.Fori(0, DEPTH) as l:
                (r1, _, _, _), (r2, _, _, _) = ffn_stages_a(l)
                sp.wait_ge(s.xn_ready1, 8 * l + 1)

                def gain():
                    broadcast(gain_a[:, :], "ffn1_norm", l * D, D, s.gain_a_landed)

                def gains():
                    broadcast(gain_m[:, :], "mix_norm", l * D, D, s.gain_m_landed)
                    broadcast(gain_f[:, :], "ffn2_norm", l * D, D, s.gain_f_landed)
                    sp.dma_start(consts_a[:, :], a["consts_a"]).then_inc(s.consts_a_landed, 16)

                def gate_biases():
                    for t in range(TT):
                        broadcast(gate[:, t, :], "mix_gate_bias", l * 2 * D, 2 * D, s.gate_bias_landed)

                def attention_bias():
                    sp.wait_ge(s.rpb_spread, LOADED * NA_DR)
                    for t in range(TT):
                        for r in range(2):
                            first = GRID_H - 1 - (2 * t + r)
                            src = bass.AP(tensor=spread.tensor,
                                          offset=l * (NA_H * NA_DR * GRID_W) + first * GRID_W,
                                          ap=[[DEPTH * NA_H * NA_DR * GRID_W, GRID_W], [NA_DR * GRID_W, NA_H], [1, T]])
                            sp.dma_start(bias[GRID_W * r:GRID_W * (r + 1), t, :, :], src).then_inc(s.bias_landed, 16)

                ffn("ffn1_w_in", "ffn1_w_out", l, r1, ((0, gain), (2, gains), (4, gate_biases), (6, attention_bias)))
                rm, _, _ = mixa_stage(l)
                for b, col in enumerate((0, 512, 1024, 1536, 2048, 2560, 3072, 3584)):
                    block_units("mix_w_in", l, A_IN, 0, col, BANK, 2 * b, rm)
                for i, name in ((16, "f_w_out"), (17, "f_w_out"), (18, "na_w_out"), (19, "na_w_out")):
                    n = i % 2
                    load(i % SLOTS, rm + i // SLOTS,
                         [rows(name, l * (BANK * D) + 2 * u * P * D + n * BANK, D, i % SLOTS, 2 * u * BANK, 2, BANK)
                          for u in range(2)])
                for n in range(2):
                    block_units("mix_w_o", l, D, 0, n * BANK, BANK, 20 + 2 * n, rm)
                ffn("ffn2_w_in", "ffn2_w_out", l, r2)

            sp.wait_ge(s.xn_ready1, 8 * DEPTH - 1)
            broadcast(gain_m[:, :], "final_norm", 0, D, s.gain_m_landed)
            sp.dma_start(consts_b[:, 0:CB_COLS], a["consts_b"]).then_inc(s.consts_b_landed, 16)

            with sp.Fori(0, DEPTH) as l:
                rm, _, _ = mixb_stage(l)
                sp.wait_ge(s.xn_ready1, 8 * DEPTH + 6 * l + 1)
                broadcast(gain_a[:, :], "attn_norm_2", l * D, D, s.gain_a_landed)
                block_units("w_in_2", l, B_IN, 0, 0, C_COLS, 0, rm)
                broadcast(gain_f[:, :], "ffn_norm_2", l * D, D, s.gain_f_landed)
                broadcast(small[:, 0:QR], "mla_q_norm_2", l * QR, QR, s.small_landed)
                broadcast(small[:, kvg_at:kvg_at + KVR], "mla_kv_norm_2", l * KVR, KVR, s.small_landed)
                broadcast(small[:, convw_at:convw_at + CONV_W * GD], "conv_w_2", l * CONV_W * GD, CONV_W * GD, s.small_landed)
                broadcast(small[:, pscale_at:pscale_at + GD], "pool_scale_2", l * GD, GD, s.small_landed)
                broadcast(small[:, sink_at:sink_at + SW_H], "swa_sinks_2", l * SW_H, SW_H, s.small_landed)
                block_units("w_in_2", l, B_IN, 0, 1440, BANK, 2, rm)
                nq = MLA_H * MLA_D
                load(4 % SLOTS, rm + 1, [rows("w_uq_2", l * (QR * nq) + k * P * nq, nq, 1, k * nq, 1, nq) for k in range(2)])
                load(5 % SLOTS, rm + 1, [rows("w_ukv_2", l * (KVR * BANK) + u * 256, BANK, 2, u * 256, 1, 256) for u in range(2)])
                block_units("w_in_2", l, B_IN, 0, 928, BANK, 6, rm)
                load(8 % SLOTS, rm + 2, [
                    (raw[0:PC, 2, u * 2 * PC:(u + 1) * 2 * PC].rearrange("p (g n) -> p g n", g=2),
                     dram("pool_w_2", l * (4 * PC * PC) + u * 2 * PC * PC, (PC, PC), (PC * PC, 2), (1, PC))) for u in range(2)])
                sp.wait_ge(x_written[1], LOADED + 14)
                broadcast(gain_m[:, :], "mix_norm_2", l * D, D, s.gain_m_landed)
                block_units("w_in_2", l, B_IN, 0, 416, BANK, 9, rm)
                for i in range(4):
                    slot, at = (11 + i) % SLOTS, (2 * l + 1 - i // 2) * (4 * P * D) + (i % 2) * BANK
                    load(slot, rm + (11 + i) // SLOTS,
                         [rows("w_o_2", at + 2 * u * P * D, D, slot, 2 * u * BANK, 2, BANK) for u in range(2)])
                rf, _, _, _ = ffn_stage_b(l)
                ffn("w_gate_up_2", "w_down_2", l, rf)

            sp.wait_ge(s.xn_ready1, 8 * DEPTH + 6 * DEPTH - 1)
            broadcast(gain_m[:, :], "final_norm_2", 0, D, s.gain_m_landed)
            last_round = B_START + DEPTH * B_ROUNDS - 1
            for slot in range(2):
                sp.wait_ge(s.w_lo_ready, unit(slot, last_round) + 4)
                sp.sem_inc(raw_landed[slot], 32)
            for t in range(TT):
                sp.wait_ge(s.final_done, t + 1)
                sp.dma_start(out[0, tok(t), :], xn[:, t, :]).then_inc(s.out_stored, 16)
            sp.wait_ge(s.out_stored, 16 * TT)

        @block.gpsimd
        def _(pool):
            pool.memset(ident[:, :], 0.0).then_inc(s.ident_zero, 1)
            pool.memset(eps[:, :], EPS)
            pool.memset(neghalf[:, :], -0.5).then_inc(s.half_ready, 1)
            pool.wait_ge(s.ident_zero, 1)
            pool.affine_select(out=ident[:, :], in_=ident[:, :], compare_op=ALU.not_equal, fill=1.0, base=0,
                               pattern=[[-1, P]], channel_multiplier=1).then_inc(s.ident_ready, 1)
            pool.wait_ge(s.half_ready, 1)

            def rsqrt(mean, sums, result, n, ready, ms_sem, out_sem, count):
                pool.wait_ge(ready, count)
                pool.tensor_tensor(sums, mean, eps[:, 0:n], ALU.add).then_inc(ms_sem, 1)
                pool.wait_ge(ms_sem, count)
                pool.tensor_tensor(result, sums, neghalf[:, 0:n], ALU.pow).then_inc(out_sem, 1)

            def norm(n):
                for t in range(TT):
                    rsqrt(ss[:, t:t + 1], ms[:, t:t + 1], rstd[:, t:t + 1], 1, s.sq_ready, s.ms_ready, s.rstd_ready,
                          2 * n + t + 1)

            def spread_table():
                with nc.allow_non_contiguous_dma(reason="rows of 64 keys"):
                    for dr in range(NA_DR):
                        src = bass.AP(tensor=a["na_rpb"].tensor, offset=(dr + 8 - GRID_H) * RPB_C + RPB_C // 2,
                                      ap=[[RPB_R * RPB_C, DEPTH * NA_H], [-1, GRID_W], [1, GRID_W]])
                        pool.dma_start(spread[:, :, dr * GRID_W:(dr + 1) * GRID_W].rearrange("q h k -> h q k"), src)\
                            .then_inc(s.rpb_spread, LOADED)

            pool.wait_ge(raw_landed[1], 2 * LOADED)
            spread_table()
            with pool.Fori(0, DEPTH) as l:
                norm(3 * l)
                pool.wait_ge(s.bias_landed, 64 * l + 64)
                pool.wait_ge(s.consts_a_landed, 16 * l + 16)
                flat = bias.rearrange("p t h k -> p (t h) k")
                pool.tensor_tensor(flat, flat, consts_a[:, CA_MASK:].unsqueeze(1).to_broadcast([P, TT * NA_H, T]),
                                   ALU.add).then_inc(s.bias_masked, 1)
                norm(3 * l + 1)
                pool.wait_ge(s.uf_sb, 2 * l + 2)
                pool.tensor_tensor(uf_parts[1], uf[:, 0, :], uf[:, 1, :], ALU.subtract).then_inc(s.uf_diff, 1)
                pool.wait_ge(s.uf_diff, l + 1)
                pool.tensor_tensor(uf_parts[0], uf[:, 0, :], uf[:, 1, :], ALU.add).then_inc(s.uf_sum, 1)
                norm(3 * l + 2)
            norm(6)
            with pool.Fori(0, DEPTH) as l:
                norm(7 + 2 * l)
                for t in range(TT):
                    rsqrt(c_ss[:, t, :], c_m[:, t, :], c_r[:, t, :], 2, s.c_sq, s.c_ms, s.c_rstd, 2 * l + t + 1)
                pool.wait_ge(s.consts_b_landed, 16)
                for t in range(TT):
                    kr = c_nat[:, t, QR + KVR:C_COLS]
                    h = ROPE // 2
                    pool.tensor_tensor(krA[:, t, :], kr, rope_table(t, 0), ALU.mult)
                    pool.tensor_tensor(krB[:, t, 0:h], kr[:, h:], rope_table(t, 1)[:, 0:h], ALU.mult)
                    pool.tensor_tensor(krB[:, t, h:], kr[:, 0:h], rope_table(t, 1)[:, h:], ALU.mult).then_inc(s.krot_a, 1)
                    pool.wait_ge(s.krot_a, 2 * l + t + 1)
                    dst = mk[:, t, :].rearrange("p (h c) -> p h c", h=MLA_H)[:, :, NOPE:]
                    pool.tensor_tensor(dst, krA[:, t, :].unsqueeze(1).to_broadcast([P, MLA_H, ROPE]),
                                       krB[:, t, :].unsqueeze(1).to_broadcast([P, MLA_H, ROPE]), ALU.add).then_inc(s.krot_ready, 1)
                pool.wait_ge(s.small_landed, 80 * l + 80)
                for t in range(TT):
                    pool.wait_ge(s.z_ready, 2 * l + t + 1)
                    taps = small[:, convw_at:convw_at + CONV_W * GD].rearrange("p (i c) -> p i c", i=CONV_W)
                    pool.tensor_tensor(zw[:, t, :, :], z[:, t, :].unsqueeze(1).to_broadcast([P, CONV_W, GD]), taps,
                                       ALU.mult).then_inc(s.zw_ready, 1)
                    pool.wait_ge(s.gsq_ready, 8 * l + 4 * t + 4)
                    pool.tensor_tensor(g_m[:, t, :], g_ss[:, t, :], eps[:, 0:4], ALU.add).then_inc(s.gms_ready, 1)
                    pool.wait_ge(s.gms_ready, 2 * l + t + 1)
                    pool.tensor_tensor(g_r[:, t, :], g_m[:, t, :], neghalf[:, 0:4], ALU.pow).then_inc(s.grstd_ready, 1)
                norm(7 + 2 * l + 1)
            norm(11)

        @block.scalar
        def _(act_e):
            act_e.wait_ge(s.half_ready, 1)
            act_e.activation(warm[:, :], neghalf[:, 0:1], ACT.Copy)

            def refill(slot, rnd):
                u = unit(slot, rnd)
                act_e.wait_ge(s.unit_done, u + 1)
                act_e.wait_ge(raw_landed[slot], 32 * (rnd + 1))
                act_e.activation(whi[:, slot, :], raw[:, slot, :], ACT.Copy).then_inc(s.w_hi_ready, 1)

            def squares(n, t):
                act_e.wait_ge(x_written[t], LOADED + 2 * n)
                if t == 1:
                    act_e.wait_ge(s.sq_ready, 2 * n + 1)
                act_e.activation(squared, x[:, t, :], ACT.Square, scale=D ** -0.5,
                                 accum_out=ss[:, t:t + 1]).then_inc(s.sq_ready, 1)

            def transposed_hi(t, o):
                for b in range(2):
                    act_e.wait_ge(s.tr_done, 4 * o + 2 * t + b + 1)
                    act_e.activation(xTh[:, 4 * b:4 * b + 4, tok(t)], pg[b][t][:, :].rearrange("p (c n) -> p c n", c=4),
                                     ACT.Copy).then_inc(s.xT_hi_ready, 1)

            def begin(rnd, n, o):
                refill(1, rnd)
                transposed_hi(0, o)
                squares(n, 0)
                refill(2, rnd)
                transposed_hi(1, o)
                squares(n, 1)
                act_e.wait_ge(s.rstd_ready, 2 * n + 2)

            def ffn(rnd, f, n, o):
                begin(rnd, n, o)

                def silu(t, par):
                    act_e.activation(sg[:, t, :], pg[par][t][:, 0:FB], ACT.Silu, scale=rstd[:, t:t + 1]).then_inc(s.silu_ready, 1)

                act_e.wait_ge(s.ffn_t0_done, STEPS * f + 1)
                silu(0, 0)
                refill(0, rnd + 1)
                act_e.wait_ge(s.unit_done, unit(1, rnd) + 4)
                silu(1, 0)

                def product_hi(j, par):
                    act_e.wait_ge(s.actT_tr, STEPS * f + j + 1)
                    act_e.activation(bTh[:, 2 * par:2 * par + 2, :], pg[par][0][:, :].rearrange("p (c n) -> p c n", c=2),
                                     ACT.Copy).then_inc(s.actT_hi, 1)

                with act_e.Fori(0, (STEPS - 1) // 2) as jj:
                    for par in range(2):
                        j = 2 * jj + par
                        product_hi(j, par)
                        refill(1, rnd + j + 1)
                        act_e.wait_ge(s.ffn_t0_done, STEPS * f + j + 2)
                        silu(0, 1 - par)
                        refill(2, rnd + j + 1)
                        act_e.wait_ge(s.unit_done, unit(0, rnd + j + 1) + 4)
                        silu(1, 1 - par)
                        refill(0, rnd + j + 2)
                product_hi(STEPS - 1, 0)

            def copy(dst, src, sem, scale=1.0):
                act_e.activation(dst, src, ACT.Copy, scale=scale).then_inc(sem, 1)

            def mixer_a(l):
                rnd, r, o = mixa_stage(l)
                begin(rnd, r, o)

                def refills(*units):
                    for i in units:
                        refill(i % SLOTS, rnd + i // SLOTS)

                def block_done(b, t):
                    if t == 0:
                        act_e.wait_ge(s.mixa_t0_done, 14 * l + b + 1)
                    else:
                        act_e.wait_ge(s.unit_done, unit(0, rnd) + 2 * b + 1 + 4)

                for b, (dst, sem) in enumerate(((q_nat, s.qk_sb), (k_nat, s.qk_sb), (v_nat, s.v_sb))):
                    for t in range(TT):
                        block_done(b, t)
                        copy(dst[:, t, :], pg[b % 2][t][:, :], sem, rstd[:, t:t + 1])
                        if t == 0:
                            refills(2 * b + 3)
                        elif b < 2:
                            refills(2 * b + 4)

                def probs_T(i):
                    act_e.wait_ge(s.naPT_done, 8 * l + i + 1)
                    copy(probsT[:, i % 2, :], acc[2][:, :], s.naPT_sb)

                def sigmoid(g, t):
                    act_e.wait_ge(s.gate_added, 8 * l + 2 * g + t + 1)
                    part = gate[:, t, g * BANK:(g + 1) * BANK]
                    act_e.activation(part, part, ACT.Sigmoid).then_inc(s.gate_sig, 1)

                for i in range(10):
                    if i < 9:
                        refills(i + 8)
                    if i < 2:
                        block_done(3, i)
                        copy(uf[:, i, :], pg[1][i][:, :], s.uf_sb, rstd[:, i:i + 1])
                    if 1 <= i <= 8:
                        probs_T(i - 1)
                    if i < 8:
                        act_e.wait_ge(s.na_negmax, 8 * l + i + 1)
                        t, hp = i // 4, i % 4
                        for e in range(2):
                            h = 4 * (hp // 2) + hp % 2 + 2 * e
                            part = probs[:, i % 2, e * T:(e + 1) * T]
                            last = act_e.activation(part, part, ACT.Exp, bias=na_neg[:, i, e:e + 1],
                                                    accum_out=na_sum[:, t, h:h + 1])
                        last.then_inc(s.na_exp, 1)
                    if i >= 2:
                        g = (i - 2) // 2
                        if i % 2 == 0:
                            act_e.wait_ge(s.dft1_done, 4 * l + g + 1)
                            copy(dft.rearrange("p (c i odd) -> p odd c i", c=2, odd=2),
                                 acc[1][:, :].rearrange("p (odd c i) -> p odd c i", c=2, odd=2), s.dft1_sb)
                        else:
                            act_e.wait_ge(s.dft2_done, 4 * l + g + 1)
                            copy(fTh[:, g, :], acc[1][:, 0:T], s.fT_hi)
                    if i == 8:
                        for g in range(3):
                            for t in range(TT):
                                sigmoid(g, t)
                for t in range(TT):
                    sigmoid(3, t)
                refills(17, 18, 19)
                for t in range(TT):
                    act_e.wait_ge(s.oT_tr, 2 * l + t + 1)
                    copy(oTh[:, :, tok(t)], acc[2 * t][:, :].rearrange("p (c n) -> p c n", c=4), s.oT_hi)
                refills(20, 21)
                transposed_hi(0, o + 1)
                transposed_hi(1, o + 1)
                refills(22, 23, 24)

            def mixer_b(l):
                rnd, r, o = mixb_stage(l)
                begin(rnd, r, o)

                def refills(*units):
                    for i in units:
                        refill(i % SLOTS, rnd + i // SLOTS)

                def done(b, i, t):
                    if t == 0:
                        act_e.wait_ge(s.mixb_t0_done, 8 * l + b + 1)
                    else:
                        act_e.wait_ge(s.unit_done, unit(0, rnd) + i + 4)

                for t in range(TT):
                    done(0, 1, t)
                    copy(c_nat[:, t, :], pg[0][t][:, 0:C_COLS], s.c_sb, rstd[:, t:t + 1])
                    act_e.wait_ge(s.c_sb, 2 * l + t + 1)
                    act_e.activation(xn[:, t, 0:QR], c_nat[:, t, 0:QR], ACT.Square, scale=QR ** -0.5, accum_out=c_ss[:, t, 0:1])
                    act_e.activation(xn[:, t, QR:QR + KVR], c_nat[:, t, QR:QR + KVR], ACT.Square, scale=KVR ** -0.5,
                                     accum_out=c_ss[:, t, 1:2]).then_inc(s.c_sq, 1)
                    refills(3 + t)

                def sw_copy(t):
                    done(1, 3, t)
                    copy(sw_nat[:, t, :], pg[1][t][:, :], s.sw_sb, rstd[:, t:t + 1])

                sw_copy(0)
                for t in range(TT):
                    act_e.wait_ge(s.cT_tr, 2 * l + t + 1)
                    copy(cTh[:, :, tok(t)], acc[t][:, 0:3 * P].rearrange("p (c n) -> p c n", c=3), s.cT_hi)
                refills(5, 6)
                sw_copy(1)
                for t in range(TT):
                    done(3, 5, t)
                    heads = acc[2 + t][:, :].rearrange("p (h c) -> p h c", h=MLA_H)
                    act_e.activation(mk[:, t, :].rearrange("p (h c) -> p h c", h=MLA_H)[:, :, 0:NOPE], heads[:, :, 0:NOPE], ACT.Copy)
                    copy(mv[:, t, :].rearrange("p (h c) -> p h c", h=MLA_H), heads[:, :, NOPE:], s.knope_sb)
                refills(7, 8)
                for t in range(TT):
                    act_e.wait_ge(s.swqT_tr, 2 * l + t + 1)
                    copy(sqT[0:SW_D, :, tok(t)], acc[2 + t][0:SW_D, :].rearrange("p (h n) -> p h n", h=SW_H), s.swqT_sb)
                act_e.wait_ge(s.swkT_tr, l + 1)
                copy(skT[0:SW_D, :, :], pg[1][0][0:SW_D, :].rearrange("p (h n) -> p h n", h=SW_KV), s.swkT_sb)

                def in_copy(t):
                    done(4, 7, t)
                    copy(conv_pool_in[:, t, :], pg[0][t][:, :], s.in_sb, rstd[:, t:t + 1])

                def sw_exp(i):
                    n, keys, h0, t = units_b[i]
                    act_e.wait_ge(s.sw_sinkarg, 3 * l + i + 1)
                    for e in range(n):
                        part = sP[:, e * keys:(e + 1) * keys]
                        last = act_e.activation(part, part, ACT.Exp, bias=s_neg[:, i, e:e + 1],
                                                accum_out=s_sum[:, t, h0 + e:h0 + e + 1])
                    last.then_inc(s.sw_exp, 1)
                    act_e.activation(s_snk[:, i, 0:n], s_arg[:, i, 0:n], ACT.Exp).then_inc(s.sw_sinkexp, 1)

                def mla_exp(i):
                    n, keys, h0, t = units_b[i]
                    act_e.wait_ge(s.mla_negmax, 3 * l + i + 1)
                    for e in range(n):
                        part = mP[:, e * keys:(e + 1) * keys]
                        last = act_e.activation(part, part, ACT.Exp, bias=m_neg[:, i, e:e + 1],
                                                accum_out=m_sum[:, t, h0 + e:h0 + e + 1])
                    last.then_inc(s.mla_exp, 1)

                def sw_probs_T(i):
                    act_e.wait_ge(s.swPT_done, 3 * l + i + 1)
                    copy(sPT, acc[2][:, :], s.swPT_sb)

                def mla_probs_T(i):
                    act_e.wait_ge(s.mlaPT_done, 3 * l + i + 1)
                    copy(mPT, acc[2][:, :], s.mlaPT_sb)

                def out_gate_copy(t):
                    done(5, 10, t)
                    copy(out_gate[:, t, :], pg[1][t][:, 0:GD], s.out_gate_sb, rstd[:, t:t + 1])

                def group_square(n, g, t, ready, count):
                    act_e.wait_ge(ready, count)
                    if n >= 2:
                        act_e.wait_ge(s.gsq_ready, 8 * l + n - 1)
                    pair = int(g in pairs_b[1])
                    at = 2 * t + pairs_b[pair].index(g)
                    act_e.activation(group_squared[:, n % 2, :], y[:, t, g * GD:(g + 1) * GD], ACT.Square, scale=GD ** -0.5,
                                     accum_out=g_ss[:, pair, at:at + 1]).then_inc(s.gsq_ready, 1)

                def pair_hi(k, t):
                    half = 1 - k
                    act_e.wait_ge(s.tr_done, 4 * (o + 1) + 2 * k + t + 1)
                    act_e.activation(xTh[:, 4 * half:4 * half + 4, tok(t)], pair_bank(t)[:, :].rearrange("p (c n) -> p c n", c=4),
                                     ACT.Copy).then_inc(s.xT_hi_ready, 1)

                in_copy(0)
                for t in range(TT):
                    act_e.wait_ge(s.mlaT_tr, 4 * l + 3 + t)
                    copy(mkT[0:MLA_D, :, tok(t)], pg[1][t][0:MLA_D, :].rearrange("p (h n) -> p h n", h=MLA_H), s.mlaT_k_sb)
                sw_exp(0)
                sw_probs_T(0)
                refills(9)
                sw_exp(1)
                mla_exp(0)
                in_copy(1)
                sw_probs_T(1)
                refills(10)
                sw_exp(2)
                mla_probs_T(0)
                mla_exp(1)
                act_e.wait_ge(s.pooled_done, l + 1)
                for b in range(2):
                    last = act_e.activation(plTh[0:PC, 2 * b:2 * b + 2, :], pg[0][b][0:PC, :].rearrange("p (g n) -> p g n", g=2), ACT.Copy)
                last.then_inc(s.pooled_hi, 1)
                out_gate_copy(0)
                sw_probs_T(2)
                group_square(0, 3, 0, s.sw_o_sb, 2 * l + 1)
                refills(11)
                group_square(1, 2, 0, s.pool_sb, l + 1)
                group_square(2, 2, 1, s.pool_sb, l + 1)
                mla_probs_T(1)
                group_square(3, 3, 1, s.sw_o_sb, 2 * l + 2)
                refills(12)
                mla_exp(2)
                out_gate_copy(1)
                mla_probs_T(2)
                group_square(4, 0, 0, s.mla_o_sb, 2 * l + 1)
                pair_hi(0, 0)
                pair_hi(0, 1)
                refills(13)
                group_square(5, 0, 1, s.mla_o_sb, 2 * l + 2)
                group_square(6, 1, 0, s.conv_sb, l + 1)
                group_square(7, 1, 1, s.conv_sb, l + 1)
                refills(14)
                pair_hi(1, 0)
                pair_hi(1, 1)
                refills(15)

            for t in range(TT):
                act_e.dma_start(x[:, t, :], bass.AP(tensor=a["x"].tensor, offset=t * P * D, ap=[[D, P], [1, D]])).then_inc(x_written[t], LOADED)
                if t == 0:
                    refill(0, 0)
            with act_e.Fori(0, DEPTH) as l:
                for m, (rnd, f, n, o) in enumerate(ffn_stages_a(l)):
                    ffn(rnd, f, n, o)
                    if m == 0:
                        mixer_a(l)
            squares(6, 0)
            squares(6, 1)
            with act_e.Fori(0, DEPTH) as l:
                mixer_b(l)
                rnd, f, n, o = ffn_stage_b(l)
                ffn(rnd, f, n, o)
            squares(11, 0)
            squares(11, 1)

        @block.vector
        def _(v):
            def refill(slot, rnd):
                v.wait_ge(s.w_hi_ready, unit(slot, rnd) + 1)
                v.tensor_tensor(wlo[:, slot, :], raw[:, slot, :], f32(whi[:, slot, :]), ALU.subtract).then_inc(s.w_lo_ready, 1)

            def operand(n, t, gain, landed, count, half=None):
                v.wait_ge(landed, count)
                for b in range(2) if half is None else (half,):
                    part = slice(b * BANK, (b + 1) * BANK)
                    v.wait_ge(x_written[t], LOADED + 2 * n - (half == 0))
                    v.tensor_tensor(xn[:, t, part], x[:, t, part], gain[:, part], ALU.mult).then_inc(xn_ready[t], 1)

            def transposed_lo(t, o, halves=(0, 1)):
                for b in halves:
                    v.wait_ge(s.xT_hi_ready, 4 * o + 2 * t + b + 1)
                    part = slice(4 * b, 4 * b + 4)
                    v.tensor_tensor(xTl[:, part, tok(t)], pg[b][t][:, :].rearrange("p (c n) -> p c n", c=4),
                                    f32(xTh[:, part, tok(t)]), ALU.subtract).then_inc(s.xT_lo_ready, 1)

            def residual(t, n, bank, factor):
                part = x[:, t, n * BANK:(n + 1) * BANK]
                v.scalar_tensor_tensor(part, bank[:, :], factor, part, ALU.mult, ALU.add).then_inc(x_written[t], 1)

            def begin(rnd, n, o, gain):
                if gain:
                    operand(n, 0, *gain)
                    transposed_lo(0, o)
                    refill(1, rnd)
                    operand(n, 1, *gain)
                    refill(2, rnd)
                transposed_lo(1, o)
                if not gain:
                    refill(2, rnd)
                v.wait_ge(s.rstd_ready, 2 * n + 2)

            def ffn(rnd, f, n, o, factor, gain=None, next_gain=None):
                begin(rnd, n, o, gain)

                def product(t, par, j):
                    v.wait_ge(s.silu_ready, 2 * STEPS * f + 2 * j + t + 1)
                    v.scalar_tensor_tensor(act[:, t, :], pg[par][t][:, FB:2 * FB], rstd[:, t:t + 1], sg[:, t, :],
                                           ALU.mult, ALU.mult).then_inc(s.act_ready, 1)

                product(0, 0, 0)
                refill(0, rnd + 1)
                product(1, 0, 0)

                def product_lo(j, par):
                    v.wait_ge(s.actT_hi, STEPS * f + j + 1)
                    part = slice(2 * par, 2 * par + 2)
                    v.tensor_tensor(bTl[:, part, :], pg[par][0][:, :].rearrange("p (c n) -> p c n", c=2),
                                    f32(bTh[:, part, :]), ALU.subtract).then_inc(s.actT_lo, 1)

                with v.Fori(0, (STEPS - 1) // 2) as jj:
                    for par in range(2):
                        j = 2 * jj + par
                        product_lo(j, par)
                        refill(1, rnd + j + 1)
                        product(0, 1 - par, j + 1)
                        refill(2, rnd + j + 1)
                        product(1, 1 - par, j + 1)
                        refill(0, rnd + j + 2)
                product_lo(STEPS - 1, 0)

                def add(t, n2):
                    if t == 1 and n2 == 1:
                        v.wait_ge(s.unit_done, unit(2, rnd + STEPS - 1) + 4)
                    else:
                        v.wait_ge(s.ffn_sum_done, 3 * f + 2 * t + n2 + 1)
                    residual(t, n2, acc[2 * t + n2], factor)

                if not next_gain:
                    for t in range(TT):
                        for n2 in range(2):
                            add(t, n2)
                    return
                for n2 in range(2):
                    add(0, n2)
                    operand(n + 1, 0, *next_gain, half=n2)
                add(1, 0)
                operand(n + 1, 1, *next_gain, half=0)
                transposed_lo(0, o + 1, halves=(0,))
                refill(1, rnd + STEPS)
                transposed_lo(0, o + 1, halves=(1,))
                add(1, 1)
                operand(n + 1, 1, *next_gain, half=1)

            def mixer_a(l, next_gain):
                rnd, r, o = mixa_stage(l)
                begin(rnd, r, o, None)

                def refills(*units):
                    for i in units:
                        refill(i % SLOTS, rnd + i // SLOTS)

                def done(b, i, t):
                    if t == 0:
                        v.wait_ge(s.mixa_t0_done, 14 * l + b + 1)
                    else:
                        v.wait_ge(s.unit_done, unit(0, rnd) + i + 4)

                refills(3, 4, 5, 6)

                def heads_T(n, dst, t, bank):
                    v.wait_ge(s.qkT_tr, 4 * l + n + 1)
                    v.tensor_copy(dst[:, :, tok(t)], bank[:, :].rearrange("p (c n) -> p c n", c=4)).then_inc(s.qkT_sb, 1)

                for n, dst in enumerate((qT, kT)):
                    for t in range(TT):
                        heads_T(2 * n + t, dst, t, acc[2 * n + t])
                refills(7)
                v.wait_ge(s.bias_masked, l + 1)
                v.wait_ge(s.gate_bias_landed, 32 * l + 32)

                def add_gate_bias(g, t):
                    done(4 + g, 2 * (4 + g) + 1, t)
                    part = gate[:, t, g * BANK:(g + 1) * BANK]
                    v.scalar_tensor_tensor(part, pg[g % 2][t][:, :], rstd[:, t:t + 1], part, ALU.mult, ALU.add).then_inc(s.gate_added, 1)

                def softmax_max(i):
                    t, hp = i // 4, i % 4
                    h = 4 * (hp // 2) + hp % 2
                    v.wait_ge(s.na_scores, 8 * l + i + 1)
                    p3 = probs[:, i % 2, :].rearrange("p (e k) -> p e k", e=2)
                    v.scalar_tensor_tensor(p3, acc[0][:, :].rearrange("p (e k) -> p e k", e=2), NA_SCALE, bias[:, t, h:h + 3:2, :],
                                           ALU.mult, ALU.add).then_inc(s.na_biased, 1)
                    v.wait_ge(s.na_biased, 8 * l + i + 1)
                    v.tensor_reduce(na_neg[:, i, :], p3, AX.X, ALU.max, negate=True).then_inc(s.na_negmax, 1)

                def normalise(t):
                    v.wait_ge(s.na_exp, 8 * l + 4 * t + 4)
                    v.reciprocal(na_inv[:, t, :], na_sum[:, t, :]).then_inc(s.na_rinv, 1)
                    v.wait_ge(s.na_rinv, 2 * l + t + 1)
                    v.wait_ge(s.na_o_done, 8 * l + 4 * t + 4)
                    v.tensor_tensor(o_nat[:, t, :].rearrange("p (h c) -> p h c", h=NA_H),
                                    acc[3][:, :].rearrange("p (h c) -> p h c", h=NA_H),
                                    na_inv[:, t, :].unsqueeze(2).to_broadcast([P, NA_H, NA_D]), ALU.mult).then_inc(s.na_o_sb, 1)

                for i in range(10):
                    if i == 6:
                        normalise(0)
                    if i < 9:
                        refills(i + 8)
                    if i >= 2:
                        add_gate_bias((i - 2) // 2, i % 2)
                    if i < 8:
                        softmax_max(i)
                    if i >= 2 and i % 2 == 1:
                        g = (i - 2) // 2
                        v.wait_ge(s.fT_hi, 4 * l + g + 1)
                        v.tensor_tensor(fTl[:, g, :], acc[1][:, 0:T], f32(fTh[:, g, :]), ALU.subtract).then_inc(s.fT_lo, 1)

                def mixed(n, t, g):
                    return gate[:, t, g * D + n * BANK:g * D + (n + 1) * BANK]

                def from_fourier(n, t):
                    done(8 + n, 16 + n, t)
                    v.wait_ge(s.gate_sig, 8 * l + 8)
                    v.tensor_tensor(xn[:, t, n * BANK:(n + 1) * BANK], pg[n][t][:, :], mixed(n, t, 1), ALU.mult)\
                        .then_inc(s.mix_f_ready, 1)

                def from_attention(n, t):
                    done(10 + n, 18 + n, t)
                    part = mixed(n, t, 0)
                    v.tensor_tensor(part, acc[(1, 3, 0, 2)[2 * n + t]][:, :], part, ALU.mult).then_inc(s.mix_na_ready, 1)
                    v.wait_ge(s.mix_na_ready, 4 * l + 2 * n + t + 1)
                    v.wait_ge(s.mix_f_ready, 4 * l + 4)
                    full = xn[:, t, n * BANK:(n + 1) * BANK]
                    v.tensor_tensor(full, full, part, ALU.add).then_inc(xn_ready[t], 1)

                normalise(1)
                refills(17, 18)
                from_fourier(0, 0)
                from_fourier(0, 1)
                refills(19)
                for t in range(TT):
                    v.wait_ge(s.oT_hi, 2 * l + t + 1)
                    v.tensor_tensor(oTl[:, :, tok(t)], acc[2 * t][:, :].rearrange("p (c n) -> p c n", c=4),
                                    f32(oTh[:, :, tok(t)]), ALU.subtract).then_inc(s.oT_lo, 1)
                from_fourier(1, 0)
                from_fourier(1, 1)
                refills(20)
                from_attention(0, 0)
                from_attention(0, 1)
                from_attention(1, 0)
                transposed_lo(0, o + 1, halves=(0,))
                refills(21)
                transposed_lo(0, o + 1, halves=(1,))
                from_attention(1, 1)
                transposed_lo(1, o + 1)
                refills(22)
                done(12, 21, 0)
                residual(0, 0, acc[0], 1.0)
                operand(r + 1, 0, *next_gain, half=0)
                refills(23)
                done(12, 21, 1)
                residual(1, 0, acc[2], 1.0)
                operand(r + 1, 1, *next_gain, half=0)
                refills(24)
                done(13, 23, 0)
                residual(0, 1, acc[1], 1.0)
                operand(r + 1, 0, *next_gain, half=1)
                transposed_lo(0, o + 2)
                refills(25)
                done(13, 23, 1)
                residual(1, 1, acc[3], 1.0)
                operand(r + 1, 1, *next_gain, half=1)

            def mixer_b(l, next_gain):
                rnd, r, o = mixb_stage(l)
                begin(rnd, r, o, (gain_a, s.gain_a_landed, 16 * (DEPTH + l) + 16))

                def refills(*units):
                    for i in units:
                        refill(i % SLOTS, rnd + i // SLOTS)

                def done(b, i, t):
                    if t == 0:
                        v.wait_ge(s.mixb_t0_done, 8 * l + b + 1)
                    else:
                        v.wait_ge(s.unit_done, unit(0, rnd) + i + 4)

                v.wait_ge(s.small_landed, 80 * l + 80)
                v.wait_ge(s.consts_b_landed, 16)
                refills(3)
                for t in range(TT):
                    v.wait_ge(s.c_rstd, 2 * l + t + 1)
                    for i, (c0, c1) in enumerate(((0, QR), (QR, QR + KVR))):
                        last = v.scalar_tensor_tensor(c_nat[:, t, c0:c1], c_nat[:, t, c0:c1], c_r[:, t, i:i + 1], small[:, c0:c1],
                                                      ALU.mult, ALU.mult)
                    last.then_inc(s.cn_ready, 1)
                refills(4)
                for t in range(TT):
                    v.wait_ge(s.cT_hi, 2 * l + t + 1)
                    v.tensor_tensor(cTl[:, :, tok(t)], acc[t][:, 0:3 * P].rearrange("p (c n) -> p c n", c=3),
                                    f32(cTh[:, :, tok(t)]), ALU.subtract).then_inc(s.cT_lo, 1)
                refills(5, 6, 7)
                for t in range(TT):
                    done(2, 4, t)
                    h2 = ROPE // 2
                    q4 = acc[t][:, 0:MLA_H * MLA_D].rearrange("p (h c) -> p h c", h=MLA_H)
                    dst = mq[:, t, :].rearrange("p (h c) -> p h c", h=MLA_H)
                    cos = rope_table(t, 0).unsqueeze(1).to_broadcast([P, MLA_H, ROPE])
                    sin = rope_table(t, 1).unsqueeze(1)
                    v.tensor_copy(dst[:, :, 0:NOPE], q4[:, :, 0:NOPE])
                    v.tensor_tensor(ropeA[:, t, :, :], q4[:, :, NOPE:], cos, ALU.mult)
                    v.tensor_tensor(ropeB[:, t, :, 0:h2], q4[:, :, NOPE + h2:], sin[:, :, 0:h2].to_broadcast([P, MLA_H, h2]), ALU.mult)
                    v.tensor_tensor(ropeB[:, t, :, h2:], q4[:, :, NOPE:NOPE + h2], sin[:, :, h2:].to_broadcast([P, MLA_H, h2]),
                                    ALU.mult).then_inc(s.rope_a, 1)
                    v.wait_ge(s.rope_a, 2 * l + t + 1)
                    v.tensor_tensor(dst[:, :, NOPE:], ropeA[:, t, :, :], ropeB[:, t, :, :], ALU.add).then_inc(s.q_sb, 1)

                def sw_max(i):
                    n, keys, h0, t = units_b[i]
                    v.wait_ge(s.sw_scores, 3 * l + i + 1)
                    v.scalar_tensor_tensor(sP, acc[1][:, :], SW_D ** -0.5, consts_b[:, CB_SWA + i * BANK:CB_SWA + (i + 1) * BANK],
                                           ALU.mult, ALU.add).then_inc(s.sw_biased, 1)
                    v.wait_ge(s.sw_biased, 3 * l + i + 1)
                    v.tensor_reduce(s_max[:, i, 0:n], sP.rearrange("p (e k) -> p e k", e=n), AX.X, ALU.max).then_inc(s.sw_max, 1)
                    v.wait_ge(s.sw_max, 3 * l + i + 1)
                    sinks = small[:, sink_at + h0:sink_at + h0 + n]
                    v.tensor_tensor(s_max[:, i, 0:n], s_max[:, i, 0:n], sinks, ALU.max).then_inc(s.sw_maxed, 1)
                    v.wait_ge(s.sw_maxed, 3 * l + i + 1)
                    v.tensor_scalar(s_neg[:, i, 0:n], s_max[:, i, 0:n], -1.0, None, ALU.mult)
                    v.tensor_tensor(s_arg[:, i, 0:n], sinks, s_max[:, i, 0:n], ALU.subtract).then_inc(s.sw_sinkarg, 1)

                def mla_max(i):
                    n, keys, h0, t = units_b[i]
                    v.wait_ge(s.mla_scores, 3 * l + i + 1)
                    mask = causal[:, P:] if keys == P else causal
                    p3 = mP.rearrange("p (e k) -> p e k", e=n)
                    v.scalar_tensor_tensor(p3, acc[0][:, :].rearrange("p (e k) -> p e k", e=n), MLA_D ** -0.5,
                                           mask.unsqueeze(1).to_broadcast([P, n, keys]), ALU.mult, ALU.add).then_inc(s.mla_biased, 1)
                    v.wait_ge(s.mla_biased, 3 * l + i + 1)
                    v.tensor_reduce(m_neg[:, i, 0:n], p3, AX.X, ALU.max, negate=True).then_inc(s.mla_negmax, 1)

                def sw_out(t):
                    for i in ((0,), (1, 2))[t]:
                        n, keys, h0, _ = units_b[i]
                        v.wait_ge(s.sw_sinkexp, 3 * l + i + 1)
                        last = v.tensor_tensor(s_den[:, t, h0:h0 + n], s_sum[:, t, h0:h0 + n], s_snk[:, i, 0:n], ALU.add)
                    last.then_inc(s.sw_den, 1)
                    v.wait_ge(s.sw_den, 2 * l + t + 1)
                    v.reciprocal(s_inv[:, t, :], s_den[:, t, :]).then_inc(s.sw_rinv, 1)
                    v.wait_ge(s.sw_rinv, 2 * l + t + 1)
                    v.wait_ge(s.sw_o_done, 3 * l + (1, 3)[t])
                    v.tensor_tensor(y[:, t, 3 * GD:].rearrange("p (h c) -> p h c", h=SW_H),
                                    acc[3][:, 0:GD].rearrange("p (h c) -> p h c", h=SW_H),
                                    s_inv[:, t, :].unsqueeze(2).to_broadcast([P, SW_H, SW_D]), ALU.mult).then_inc(s.sw_o_sb, 1)

                def mla_out(t):
                    v.wait_ge(s.mla_exp, 3 * l + (1, 3)[t])
                    v.reciprocal(m_inv[:, t, :], m_sum[:, t, :]).then_inc(s.mla_rinv, 1)
                    v.wait_ge(s.mla_rinv, 2 * l + t + 1)
                    v.wait_ge(s.mla_o_done, 3 * l + (1, 3)[t])
                    v.tensor_tensor(y[:, t, 0:GD].rearrange("p (h c) -> p h c", h=MLA_H),
                                    pg[0][1][:, 0:GD].rearrange("p (h c) -> p h c", h=MLA_H),
                                    m_inv[:, t, :].unsqueeze(2).to_broadcast([P, MLA_H, MLA_V]), ALU.mult).then_inc(s.mla_o_sb, 1)

                def conv_in(t):
                    done(5, 10, t)
                    v.wait_ge(s.out_gate_sb, 2 * l + t + 1)
                    v.scalar_tensor_tensor(z[:, t, :], pg[1][t][:, GD:], rstd[:, t:t + 1], conv_pool_in[:, t, 0:GD], ALU.mult, ALU.mult)\
                        .then_inc(s.z_ready, 1)

                def scale_pair(k):
                    v.wait_ge(s.grstd_ready, 2 * l + k + 1)
                    for t in range(TT):
                        for i, g in enumerate(pairs_b[k]):
                            c = slice(g * GD, (g + 1) * GD)
                            last = v.scalar_tensor_tensor(xn[:, t, c], y[:, t, c], g_r[:, k, 2 * t + i:2 * t + i + 1], gain_m[:, c],
                                                          ALU.mult, ALU.mult)
                        last.then_inc(xn_ready[t], 1)

                def pair_lo(k, t):
                    half = 1 - k
                    part = slice(4 * half, 4 * half + 4)
                    v.wait_ge(s.xT_hi_ready, 4 * (o + 1) + 2 * k + t + 1)
                    v.tensor_tensor(xTl[:, part, tok(t)], pair_bank(t)[:, :].rearrange("p (c n) -> p c n", c=4),
                                    f32(xTh[:, part, tok(t)]), ALU.subtract).then_inc(s.xT_lo_ready, 1)

                sw_max(0)
                for t, bank in ((0, 0), (1, 2)):
                    v.wait_ge(s.mlaT_tr, 4 * l + t + 1)
                    v.tensor_copy(mqT[0:MLA_D, :, tok(t)], acc[bank][0:MLA_D, :].rearrange("p (h n) -> p h n", h=MLA_H)).then_inc(s.mlaT_q_sb, 1)
                refills(8)
                sw_max(1)
                mla_max(0)
                refills(9)
                sw_out(0)
                sw_max(2)
                refills(10)
                mla_max(1)
                v.wait_ge(s.pooled_hi, l + 1)
                for b in range(2):
                    part = slice(2 * b, 2 * b + 2)
                    last = v.tensor_tensor(plTl[0:PC, part, :], pg[0][b][0:PC, :].rearrange("p (g n) -> p g n", g=2),
                                           f32(plTh[0:PC, part, :]), ALU.subtract)
                last.then_inc(s.pooled_lo, 1)
                conv_in(0)
                mla_out(0)
                v.wait_ge(s.unit_done, unit(0, rnd) + 8 + 4)
                v.tensor_tensor(y[:, :, 2 * GD:3 * GD], pg[0][0][:, :].rearrange("p (t c) -> p t c", t=TT),
                                small[:, pscale_at:pscale_at + GD].unsqueeze(1).to_broadcast([P, TT, GD]), ALU.mult).then_inc(s.pool_sb, 1)
                refills(11)
                sw_out(1)
                mla_max(2)
                refills(12)
                conv_in(1)
                v.wait_ge(s.gain_m_landed, 16 * (DEPTH + 1) + 16 * l + 16)
                scale_pair(0)
                mla_out(1)
                pair_lo(0, 0)
                pair_lo(0, 1)
                refills(13)
                v.wait_ge(s.conv_done, l + 1)
                v.tensor_tensor(y[:, :, GD:2 * GD], pg[1][1][:, :].rearrange("p (t c) -> p t c", t=TT), out_gate[:, :, :],
                                ALU.mult).then_inc(s.conv_sb, 1)
                scale_pair(1)
                refills(14)
                pair_lo(1, 0)
                pair_lo(1, 1)
                for n in range(2):
                    for t in range(TT):
                        done(6 + n, 13 + n, t)
                        residual(t, n, out_b[n][t], 1.0)
                        operand(r + 1, t, *next_gain, half=n)
                        if t == 0 and n == 0:
                            refills(15)
                        if t == 0 and n == 1:
                            transposed_lo(0, o + 2, halves=(0,))
                            refills(16)
                            transposed_lo(0, o + 2, halves=(1,))

            def final(n, count, dst, sems, step):
                v.wait_ge(s.gain_m_landed, count)
                for t in range(TT):
                    v.wait_ge(s.rstd_ready, 2 * n + t + 1)
                    v.scalar_tensor_tensor(dst[:, t, :], x[:, t, :], rstd[:, t:t + 1], gain_m[:, :], ALU.mult, ALU.mult)\
                        .then_inc(sems[t], step)

            v.sem_inc(s.w_lo_ready, SLOTS)
            for t in range(TT):
                v.sem_inc(xn_ready[t], 1)
            refill(0, 0)
            with v.Fori(0, DEPTH) as l:
                (first, second) = ffn_stages_a(l)
                ffn(*first, 0.5, gain=(gain_a, s.gain_a_landed, 16 * l + 16), next_gain=(gain_m, s.gain_m_landed, 16 * l + 16))
                mixer_a(l, (gain_f, s.gain_f_landed, 16 * l + 16))
                ffn(*second, 0.5)
            final(6, 16 * (DEPTH + 1), x, x_written, 2)
            with v.Fori(0, DEPTH) as l:
                mixer_b(l, (gain_f, s.gain_f_landed, 16 * (DEPTH + l) + 16))
                ffn(*ffn_stage_b(l), 1.0)
            final(11, 16 * (2 * DEPTH + 2), xn, (s.final_done, s.final_done), 1)

        @block.tensor
        def _(pe):
            def product(dst, pairs, first=True, last=True):
                for i, (xh, xl, wh, wl) in enumerate(pairs):
                    pe.matmul(dst, xh, wh, start=first and i == 0, stop=False)
                    pe.matmul(dst, xh, wl, start=False, stop=False)
                    mm = pe.matmul(dst, xl, wh, start=False, stop=last and i == len(pairs) - 1)
                return mm

            def weights(slot, at, n):
                return whi[:, slot, at:at + n], wlo[:, slot, at:at + n]

            def transposes(t, b, o):
                pe.wait_ge(xn_ready[t], 2 * o + b + 2)
                for c in range(4):
                    at = (4 * b + c) * P
                    tr = pe.transpose(pg[b][t][:, c * P:(c + 1) * P], xn[:, t, at:at + P], ident[:, :])
                tr.then_inc(s.tr_done, 1)

            def operand_ready(t, b, o):
                pe.wait_ge(s.xT_lo_ready, 4 * o + 2 * t + b + 1)

            def split_ready(slot, rnd):
                pe.wait_ge(s.w_lo_ready, unit(slot, rnd) + 4)

            def half_block(t, half, slot, rnd, n, bank, amid=None, first=0):
                if t == 0:
                    split_ready(slot, rnd)
                for k0 in range(0, 4, 2):
                    if k0 and amid:
                        amid()
                    pairs = [(xTh[:, 4 * half + k, tok(t)], xTl[:, 4 * half + k, tok(t)], *weights(slot, k * n, n)) for k in (k0, k0 + 1)]
                    mm = product(bank[:, 0:n], pairs, first=half == first and k0 == 0, last=half != first and k0 == 2)
                return mm

            def full_block(slots, rnds, n, banks, t0_sem, before=None, amid=None):
                for t in range(TT):
                    for half in range(2):
                        if before and (t, half) in before:
                            before[t, half]()
                        mm = half_block(t, half, slots[half], rnds[half], n, banks[t], (amid or {}).get((t, half)))
                        if t == 1:
                            mm.then_inc(s.unit_done, 1)
                    if t == 0:
                        mm.then_inc(t0_sem, 1)

            def first_block(slots, rnds, n, banks, t0_sem, o):
                operand_ready(0, 0, o)
                half_block(0, 0, slots[0], rnds[0], n, banks[0])
                transposes(1, 0, o)
                operand_ready(0, 1, o)
                half_block(0, 1, slots[1], rnds[1], n, banks[0], amid=lambda: transposes(1, 1, o)).then_inc(t0_sem, 1)
                for half in range(2):
                    operand_ready(1, half, o)
                    half_block(1, half, slots[half], rnds[half], n, banks[1]).then_inc(s.unit_done, 1)

            def first_tile(o):
                for b in range(2):
                    transposes(0, b, o)

            def ffn(rnd, f, n, o, alone):
                if alone[0]:
                    first_tile(o)
                first_block((0, 1), (rnd, rnd), BANK, pg[0], s.ffn_t0_done, o)

                def turn(j, par):
                    pe.wait_ge(s.act_ready, 2 * STEPS * f + 2 * j + 2)
                    for t in range(TT):
                        for c in range(2):
                            tr = pe.transpose(pg[par][0][:, c * T + t * P:c * T + (t + 1) * P], act[:, t, c * P:(c + 1) * P], ident[:, :])
                    tr.then_inc(s.actT_tr, 1)

                def added(t, par, slot, n2, k, first, last):
                    return product(acc[2 * t + n2][:, :], [(bTh[:, 2 * par + k, tok(t)], bTl[:, 2 * par + k, tok(t)],
                                                            *weights(slot, k * D + n2 * BANK, BANK))], first=first, last=last)

                def down(j, par, slot, r, first):
                    pe.wait_ge(s.actT_lo, STEPS * f + j + 1)
                    split_ready(slot, r)
                    for t in range(TT):
                        for k in range(2):
                            for n2 in range(2):
                                mm = added(t, par, slot, n2, k, first and k == 0, False)
                        if t == 0:
                            turn(j + 1, 1 - par)
                    mm.then_inc(s.unit_done, 1)

                def last_down(slot, r):
                    pe.wait_ge(s.actT_lo, STEPS * f + STEPS)
                    split_ready(slot, r)
                    for t in range(TT):
                        for n2 in range(2):
                            for k in range(2):
                                mm = added(t, 0, slot, n2, k, False, k == 1)
                            if t == 0 or n2 == 0:
                                mm.then_inc(s.ffn_sum_done, 1)
                            if t == 1:
                                if n2 == 1:
                                    mm.then_inc(s.unit_done, 1)
                                if not alone[1]:
                                    transposes(0, n2, o + 1)

                def step(j, par, amid=None, first=False):
                    full_block((2, 0), (rnd + j, rnd + j + 1), BANK, pg[1 - par], s.ffn_t0_done, amid=amid)
                    down(j, par, 1, rnd + j + 1, first)

                step(0, 0, {(0, 1): lambda: turn(0, 0)}, first=True)
                with pe.Fori(0, (STEPS - 3) // 2) as jj:
                    step(2 * jj + 1, 1)
                    step(2 * jj + 2, 0)
                step(STEPS - 2, 1)
                last_down(2, rnd + STEPS - 1)

            def mixer_a(l):
                rnd, r, o = mixa_stage(l)

                def slots(i):
                    return ((i % SLOTS, (i + 1) % SLOTS), (rnd + i // SLOTS, rnd + (i + 1) // SLOTS))

                def in_block(b, before=None):
                    full_block(*slots(2 * b), BANK, pg[b % 2], s.mixa_t0_done, before)

                first_block(*slots(0), BANK, pg[0], s.mixa_t0_done, o)
                in_block(1)

                def heads_T(src, n):
                    for t in range(TT):
                        pe.wait_ge(s.qk_sb, 4 * l + 2 * n + t + 1)
                        for c in range(4):
                            tr = pe.transpose(acc[2 * n + t][:, c * P:(c + 1) * P], src[:, t, c * P:(c + 1) * P], ident[:, :])
                        tr.then_inc(s.qkT_tr, 1)

                heads_T(q_nat, 0)
                in_block(2, {(1, 1): lambda: heads_T(k_nat, 1)})

                def scores(i):
                    t, hp = i // 4, i % 4
                    rows = slice(64 * (hp % 2), 64 * (hp % 2) + 64)
                    if i >= 1:
                        pe.wait_ge(s.na_biased, 8 * l + i)
                    else:
                        pe.wait_ge(s.qkT_sb, 4 * l + 4)
                    for e in range(2):
                        c = 2 * (hp // 2) + e
                        mm = pe.matmul(acc[0][:, e * T:(e + 1) * T], qT[rows, c, tok(t)], kT[rows, c, :], start=True, stop=True)
                    mm.then_inc(s.na_scores, 1)

                def probs_T(i):
                    pe.wait_ge(s.na_exp, 8 * l + i + 1)
                    for e in range(2):
                        for kt in range(TT):
                            at = e * T + kt * P
                            tr = pe.transpose(acc[2][:, at:at + P], probs[:, i % 2, at:at + P], ident[:, :])
                    tr.then_inc(s.naPT_done, 1)

                def attend(i):
                    t, hp = i // 4, i % 4
                    pe.wait_ge(s.naPT_sb, 8 * l + i + 1)
                    if i == 4:
                        pe.wait_ge(s.na_o_sb, 2 * l + 1)
                    for e in range(2):
                        h = 4 * (hp // 2) + hp % 2 + 2 * e
                        for kt in range(TT):
                            at = e * T + kt * P
                            mm = pe.matmul(acc[3][:, h * NA_D:(h + 1) * NA_D], probsT[:, i % 2, at:at + P],
                                           v_nat[:, kt, h * NA_D:(h + 1) * NA_D], start=kt == 0, stop=kt == 1)
                    mm.then_inc(s.na_o_done, 1)

                def dft_positions(g):
                    if g == 0:
                        pe.wait_ge(s.uf_sum, l + 1)
                        pe.wait_ge(s.consts_a_landed, 16 * l + 16)
                    else:
                        pe.wait_ge(s.fT_lo, 4 * l + g)
                    for odd in range(2):
                        at = CA_DFT_T + odd * T
                        mm = pe.matmul(acc[1][:, odd * T:(odd + 1) * T], uf_parts[odd][:, g * FC:(g + 1) * FC], consts_a[:, at:at + T],
                                       start=True, stop=True)
                    mm.then_inc(s.dft1_done, 1)

                def dft_channels(g):
                    pe.wait_ge(s.dft1_sb, 4 * l + g + 1)
                    for n in range(2):
                        mm = pe.matmul(acc[1][:, 0:T], consts_a[:, CA_DFT_C + n * FC:CA_DFT_C + (n + 1) * FC],
                                       dft[:, n * T:(n + 1) * T], start=n == 0, stop=n == 1)
                    mm.then_inc(s.dft2_done, 1)

                for i in range(10):
                    b, t = 3 + i // 2, i % 2
                    sl, rn = slots(2 * b)
                    if b >= 6 and t == 0:
                        pe.wait_ge(s.gate_added, 8 * l + 2 * (b - 5))
                    if b == 4 and t == 0:
                        pe.wait_ge(s.v_sb, 2 * l + 2)
                    if b == 5 and t == 0:
                        pe.wait_ge(s.uf_sb, 2 * l + 2)
                    for half in range(2):
                        mm = half_block(t, half, sl[half], rn[half], BANK, pg[b % 2][t])
                        if t == 1:
                            mm.then_inc(s.unit_done, 1)
                    if t == 0:
                        mm.then_inc(s.mixa_t0_done, 1)
                    if i < 8:
                        scores(i)
                    if 2 <= i:
                        attend(i - 2)
                    if 1 <= i <= 8:
                        probs_T(i - 1)
                    if i >= 2:
                        (dft_positions, dft_channels)[i % 2]((i - 2) // 2)

                def out_projection(i, idx, src_h, src_l, banks, between=None):
                    split_ready(i % SLOTS, rnd + i // SLOTS)
                    for t in range(TT):
                        if t == 1 and between:
                            between()
                        mm = product(banks[t][:, :], [(src_h[:, k, tok(t)], src_l[:, k, tok(t)], *weights(i % SLOTS, k * BANK, BANK))
                                                      for k in range(4)])
                        mm.then_inc(s.mixa_t0_done if t == 0 else s.unit_done, 1)

                def attention_T(t):
                    pe.wait_ge(s.na_o_sb, 2 * l + t + 1)
                    for c in range(4):
                        tr = pe.transpose(acc[2 * t][:, c * P:(c + 1) * P], o_nat[:, t, c * P:(c + 1) * P], ident[:, :])
                    tr.then_inc(s.oT_tr, 1)

                attention_T(0)
                pe.wait_ge(s.fT_lo, 4 * l + 4)
                pe.wait_ge(s.gate_added, 8 * l + 6)
                out_projection(16, 8, fTh, fTl, pg[0])
                attention_T(1)
                pe.wait_ge(s.gate_added, 8 * l + 8)
                out_projection(17, 9, fTh, fTl, pg[1])
                pe.wait_ge(s.oT_lo, 2 * l + 2)
                out_projection(18, 10, oTh, oTl, (acc[1], acc[3]))
                out_projection(19, 11, oTh, oTl, (acc[0], acc[2]), lambda: transposes(0, 0, o + 1))
                transposes(0, 1, o + 1)
                first_block(*slots(20), BANK, (acc[0], acc[2]), s.mixa_t0_done, o + 1)
                full_block(*slots(22), BANK, (acc[1], acc[3]), s.mixa_t0_done, {(1, 1): lambda: first_tile(o + 2)})

            def mixer_b(l):
                rnd, r, o = mixb_stage(l)

                def slots(i):
                    return ((i % SLOTS, (i + 1) % SLOTS), (rnd + i // SLOTS, rnd + (i + 1) // SLOTS))

                first_tile(o)
                first_block(*slots(0), C_COLS, pg[0], s.mixb_t0_done, o)

                def latents_T():
                    for t in range(TT):
                        pe.wait_ge(s.cn_ready, 2 * l + t + 1)
                        for c in range(3):
                            tr = pe.transpose(acc[t][:, c * P:(c + 1) * P], c_nat[:, t, c * P:(c + 1) * P], ident[:, :])
                        tr.then_inc(s.cT_tr, 1)

                full_block(*slots(2), BANK, pg[1], s.mixb_t0_done, {(1, 0): latents_T})
                pe.wait_ge(s.cT_lo, 2 * l + 2)
                split_ready(1, rnd + 1)
                nq = MLA_H * MLA_D
                for t in range(TT):
                    mm = product(acc[t][:, 0:nq], [(cTh[:, k, tok(t)], cTl[:, k, tok(t)], *weights(1, k * nq, nq)) for k in range(2)])
                    mm.then_inc(s.mixb_t0_done if t == 0 else s.unit_done, 1)
                split_ready(2, rnd + 1)
                for t in range(TT):
                    mm = product(acc[2 + t][:, :], [(cTh[:, 2, tok(t)], cTl[:, 2, tok(t)], *weights(2, 0, BANK))])
                    mm.then_inc(s.mixb_t0_done if t == 0 else s.unit_done, 1)

                def sw_operands():
                    pe.wait_ge(s.sw_sb, 2 * l + 2)
                    pe.wait_ge(s.knope_sb, 2 * l + 2)

                def sw_heads_T():
                    for t in range(TT):
                        for h in range(SW_H):
                            tr = pe.transpose(acc[2 + t][0:SW_D, h * P:(h + 1) * P], sw_nat[:, t, h * SW_D:(h + 1) * SW_D], ident[:, :])
                        tr.then_inc(s.swqT_tr, 1)
                    for t in range(TT):
                        for h in range(SW_KV):
                            at = SW_H * SW_D + h * SW_D
                            tr = pe.transpose(pg[1][0][0:SW_D, h * T + t * P:h * T + (t + 1) * P], sw_nat[:, t, at:at + SW_D], ident[:, :])
                    tr.then_inc(s.swkT_tr, 1)

                def sw_scores(i):
                    n, keys, h0, t = units_b[i]
                    if i == 0:
                        pe.wait_ge(s.q_sb, 2 * l + 2)
                        pe.wait_ge(s.swqT_sb, 2 * l + 2)
                        pe.wait_ge(s.swkT_sb, l + 1)
                    else:
                        pe.wait_ge(s.sw_biased, 3 * l + i)
                    for e in range(n):
                        mm = pe.matmul(acc[1][:, e * keys:(e + 1) * keys], sqT[0:SW_D, h0 + e, tok(t)],
                                       skT[0:SW_D, (h0 + e) // 2, 0:keys], start=True, stop=True)
                    mm.then_inc(s.sw_scores, 1)

                def mla_scores(i):
                    n, keys, h0, t = units_b[i]
                    if i == 0:
                        pe.wait_ge(s.mlaT_q_sb, 2 * l + 2)
                        pe.wait_ge(s.mlaT_k_sb, 2 * l + 2)
                    else:
                        pe.wait_ge(s.mla_biased, 3 * l + i)
                    for e in range(n):
                        mm = pe.matmul(acc[0][:, e * keys:(e + 1) * keys], mqT[0:MLA_D, h0 + e, tok(t)],
                                       mkT[0:MLA_D, h0 + e, 0:keys], start=True, stop=True)
                    mm.then_inc(s.mla_scores, 1)

                def sw_probs_T(i):
                    pe.wait_ge(s.sw_exp, 3 * l + i + 1)
                    if i == 0:
                        pe.wait_ge(s.mlaT_q_sb, 2 * l + 2)
                    if i == 1:
                        pe.wait_ge(s.swPT_sb, 3 * l + 1)
                    if i == 2:
                        pe.wait_ge(s.mlaPT_sb, 3 * l + 1)
                    for c in range(4):
                        tr = pe.transpose(acc[2][:, c * P:(c + 1) * P], sP[:, c * P:(c + 1) * P], ident[:, :])
                    tr.then_inc(s.swPT_done, 1)

                def mla_probs_T(i):
                    pe.wait_ge(s.mla_exp, 3 * l + i + 1)
                    if i < 2:
                        pe.wait_ge(s.swPT_sb, 3 * l + i + 2)
                    for c in range(4):
                        tr = pe.transpose(acc[2][:, c * P:(c + 1) * P], mP[:, c * P:(c + 1) * P], ident[:, :])
                    tr.then_inc(s.mlaPT_done, 1)

                def attend(i, bank, pT, value, sem):
                    n, keys, h0, t = units_b[i]
                    for e in range(n):
                        h = h0 + e
                        for kt in range(keys // P):
                            at = e * keys + kt * P
                            mm = pe.matmul(bank[:, h * 64:(h + 1) * 64], pT[:, at:at + P], value(kt, h), start=kt == 0, stop=kt == keys // P - 1)
                    mm.then_inc(sem, 1)

                def sw_attend(i):
                    pe.wait_ge(s.swPT_sb, 3 * l + i + 1)
                    if i == 1:
                        pe.wait_ge(s.sw_o_sb, 2 * l + 1)
                    at = (SW_H + SW_KV) * SW_D
                    attend(i, acc[3], sPT, lambda kt, h: sw_nat[:, kt, at + (h // 2) * SW_D:at + (h // 2 + 1) * SW_D], s.sw_o_done)

                def mla_attend(i):
                    pe.wait_ge(s.mlaPT_sb, 3 * l + i + 1)
                    if i == 0:
                        pe.wait_ge(s.pooled_lo, l + 1)
                    if i == 1:
                        pe.wait_ge(s.mla_o_sb, 2 * l + 1)
                    attend(i, pg[0][1], mPT, lambda kt, h: mv[:, kt, h * MLA_V:(h + 1) * MLA_V], s.mla_o_done)

                def mla_heads_T():
                    for src, banks in ((mq, (acc[0], acc[2])), (mk, pg[1])):
                        if src is mk:
                            pe.wait_ge(s.krot_ready, 2 * l + 2)
                        for t in range(TT):
                            for h in range(MLA_H):
                                tr = pe.transpose(banks[t][0:MLA_D, h * P:(h + 1) * P], src[:, t, h * MLA_D:(h + 1) * MLA_D], ident[:, :])
                            tr.then_inc(s.mlaT_tr, 1)

                def conv():
                    pe.wait_ge(s.zw_ready, 2 * l + 2)
                    pe.wait_ge(s.out_gate_sb, 2 * l + 2)

                    def shift(n):
                        return consts_b[:, CB_CONV + n * P:CB_CONV + (n + 1) * P]

                    for t in range(TT):
                        terms = [(shift(i), zw[:, t, i, :]) for i in range(CONV_W)]
                        if t == 1:
                            terms += [(shift(3 + i), zw[:, 0, i, :]) for i in range(2)]
                        for n, (m, taps) in enumerate(terms):
                            mm = pe.matmul(pg[1][1][:, t * GD:(t + 1) * GD], m, taps, start=n == 0, stop=n == len(terms) - 1)
                    mm.then_inc(s.conv_done, 1)

                def pooled():
                    pe.wait_ge(s.in_sb, 2 * l + 2)
                    for g in range(4):
                        dst = pg[0][g // 2][0:PC, (g % 2) * T:(g % 2 + 1) * T]
                        band = consts_b[:, CB_POOL + g * 3 * P:CB_POOL + (g + 1) * 3 * P]
                        chans = slice(GD + g * PC, GD + (g + 1) * PC)
                        pe.matmul(dst, conv_pool_in[:, 0, chans], band[:, 0:T], start=True, stop=False)
                        mm = pe.matmul(dst[:, P:T], conv_pool_in[:, 1, chans], band[:, T:], start=False, stop=True)
                    mm.then_inc(s.pooled_done, 1)

                def pool_mix():
                    pe.wait_ge(s.pooled_lo, l + 1)
                    split_ready(2, rnd + 2)
                    for t in range(TT):
                        for g in range(4):
                            mm = product(pg[0][0][:, t * GD + g * PC:t * GD + (g + 1) * PC],
                                         [(plTh[0:PC, g, tok(t)], plTl[0:PC, g, tok(t)],
                                           whi[0:PC, 2, g * PC:(g + 1) * PC], wlo[0:PC, 2, g * PC:(g + 1) * PC])])
                    mm.then_inc(s.unit_done, 1)

                for i in range(8):
                    b, t, half = i // 4, (i // 2) % 2, i % 2
                    u = (6, 9)[b] + half
                    mm = half_block(t, half, u % SLOTS, rnd + u // SLOTS, BANK, pg[b][t], sw_operands if i == 0 else None)
                    if t == 1:
                        mm.then_inc(s.unit_done, 1)
                    elif half == 1:
                        mm.then_inc(s.mixb_t0_done, 1)
                    if i == 0:
                        sw_heads_T()
                    if i == 1:
                        sw_scores(0)
                        mla_heads_T()
                    if i == 2:
                        mla_scores(0)
                        sw_probs_T(0)
                        sw_scores(1)
                    if i == 3:
                        sw_attend(0)
                        sw_probs_T(1)
                        sw_scores(2)
                    if i == 4:
                        mla_probs_T(0)
                        mla_scores(1)
                        sw_attend(1)
                        pooled()
                    if i == 5:
                        sw_probs_T(2)
                        mla_attend(0)
                        pool_mix()
                    if i == 6:
                        sw_attend(2)
                        mla_probs_T(1)
                        mla_scores(2)
                    if i == 7:
                        mla_attend(1)
                        mla_probs_T(2)
                mla_attend(2)

                def pair_T(k, t):
                    half = 1 - k
                    if k == 0 and t == 1:
                        pe.wait_ge(s.z_ready, 2 * l + 1)
                        pe.wait_ge(s.out_gate_sb, 2 * l + 1)
                    pe.wait_ge(xn_ready[t], 2 * (o + 1) + k + 2)
                    for c in range(4):
                        at = (4 * half + c) * P
                        tr = pe.transpose(pair_bank(t)[:, c * P:(c + 1) * P], xn[:, t, at:at + P], ident[:, :])
                    tr.then_inc(s.tr_done, 1)

                def project(i, t, amid=None):
                    k, n, u = i // 2, i % 2, 11 + i
                    if n == 0:
                        pe.wait_ge(s.xT_lo_ready, 4 * (o + 1) + 2 * k + t + 1)
                    mm = half_block(t, 1 - k, u % SLOTS, rnd + u // SLOTS, BANK, out_b[n][t], amid, first=1)
                    if t == 1:
                        mm.then_inc(s.unit_done, 1)
                    elif k == 1:
                        mm.then_inc(s.mixb_t0_done, 1)

                pair_T(0, 0)
                pair_T(0, 1)
                project(0, 0)
                conv()
                project(0, 1)
                project(1, 0)
                project(1, 1, lambda: pair_T(1, 0))
                pair_T(1, 1)
                project(2, 0)
                project(2, 1)
                project(3, 0)
                transposes(0, 0, o + 2)
                project(3, 1, lambda: transposes(0, 1, o + 2))

            pe.sem_inc(s.unit_done, SLOTS)
            pe.wait_ge(s.ident_ready, 1)
            with pe.Fori(0, DEPTH) as l:
                first, second = ffn_stages_a(l)
                ffn(*first, alone=(True, False))
                mixer_a(l)
                ffn(*second, alone=(False, True))
            with pe.Fori(0, DEPTH) as l:
                mixer_b(l)
                ffn(*ffn_stage_b(l), alone=(False, True))


INPUTS = """x ffn1_norm ffn1_w_in ffn1_w_out mix_norm mix_w_in mix_gate_bias na_rpb na_w_out f_w_out mix_w_o
ffn2_norm ffn2_w_in ffn2_w_out final_norm attn_norm_2 w_in_2 mla_q_norm_2 w_uq_2 mla_kv_norm_2 w_ukv_2 conv_w_2
pool_w_2 pool_scale_2 swa_sinks_2 mix_norm_2 w_o_2 ffn_norm_2 w_gate_up_2 w_down_2 final_norm_2""".split()


def kernel(**inputs):
    import concourse.bacc as bacc
    from concourse.bass_utils import run_bass_kernel_spmd

    nc = bacc.Bacc("TRN2", target_bir_lowering=False, num_devices=1)
    arrays = {n: np.ascontiguousarray(inputs[n]) for n in INPUTS}
    arrays["consts_a"] = first_constants()
    arrays["consts_b"] = second_constants()
    handles = {n: nc.dram_tensor(f"in_{n}", v.shape, F32, kind="ExternalInput").ap() for n, v in arrays.items()}
    out = nc.dram_tensor("out", (1, T, D), F32, kind="ExternalOutput").ap()
    build(nc, handles, out)
    r = run_bass_kernel_spmd(nc, [{f"in_{n}": v for n, v in arrays.items()}], core_ids=[0])
    return r.results[0]["out"]
```
